# Optimizing a Trainium2 kernel written in Bass

```python
import jax, jax.numpy as jnp
from jax import lax
import numpy as np

D_MODEL = 1024
BATCH = 1
SEQ = 512
DEPTH = 1
DEC_BATCH = 8
DEC_SEQ = 4
PAST_LEN = 4096
PAGE_SIZE = 128

MIX_WIDTH = D_MODEL
POOL_WIDTH = MIX_WIDTH // 2
POOL_WINDOWS = (2, 4, 8, 16)
POOL_GROUPS = len(POOL_WINDOWS)
POOL_GROUP_DIM = POOL_WIDTH // POOL_GROUPS
POOL_BUF = max(POOL_WINDOWS) - 1
SGU_WIDTH = MIX_WIDTH - POOL_WIDTH
SGU_HEADS = 4
SGU_HEAD_DIM = SGU_WIDTH // SGU_HEADS
CHUNK = 128
IN_WIDTH = POOL_WIDTH + 2 * SGU_WIDTH
N_EXPERTS = 32
TOP_K = 4
D_FF = D_MODEL
SWIGLU_LIMIT = 7.0
SWIGLU_ALPHA = 1.702
MOE_BLOCK = 128
PLE_DIM = 256
RMS_EPS = 1e-6
LN_EPS = 1e-5

kernel_name = "hybrid_pool_sgu_moe_decoder_step"

def rmsnorm(x, g):
    xf = x.astype(jnp.float32)
    y = xf * lax.rsqrt(jnp.mean(xf * xf, axis=-1, keepdims=True) + RMS_EPS)
    return (y * g.astype(jnp.float32)).astype(x.dtype)

def head_layernorm(v, g, b):
    vf = v.astype(jnp.float32)
    mu = jnp.mean(vf, axis=-1, keepdims=True)
    var = jnp.mean(jnp.square(vf - mu), axis=-1, keepdims=True)
    y = (vf - mu) * lax.rsqrt(var + LN_EPS) * g.astype(jnp.float32) + b.astype(jnp.float32)
    return y.astype(v.dtype)

def pool_mix(z, prefix, pos0, w_pool, pool_scale):
    B, L, _ = z.shape
    ext = jnp.concatenate([prefix.astype(z.dtype), z], axis=1)
    cs = jnp.cumsum(ext.astype(jnp.float32), axis=1)
    cs = jnp.pad(cs, ((0, 0), (1, 0), (0, 0)))
    pos = pos0 + jnp.arange(L)
    outs = []
    for g, w in enumerate(POOL_WINDOWS):
        cols = slice(g * POOL_GROUP_DIM, (g + 1) * POOL_GROUP_DIM)
        hi = cs[:, POOL_BUF + 1:POOL_BUF + 1 + L, cols]
        lo = cs[:, POOL_BUF + 1 - w:POOL_BUF + 1 - w + L, cols]
        cnt = jnp.minimum(w, pos + 1).astype(jnp.float32)[None, :, None]
        outs.append((hi - lo) / cnt)
    pooled = jnp.stack(outs, axis=2)
    diff = pooled - z.astype(jnp.float32).reshape(B, L, POOL_GROUPS, POOL_GROUP_DIM)
    y = jnp.einsum('blgc,gcd->blgd', diff.astype(z.dtype), w_pool) * pool_scale
    return y.reshape(B, L, POOL_WIDTH), ext[:, -POOL_BUF:]

def sgu_mix(v, w_s, b_s):
    B, L, H, dh = v.shape
    n_chunks = -(-L // CHUNK)
    pad = n_chunks * CHUNK - L
    vp = jnp.pad(v, ((0, 0), (0, pad), (0, 0), (0, 0))).reshape(B, n_chunks, CHUNK, H, dh)
    mask = jnp.tril(jnp.ones((CHUNK, CHUNK), dtype=bool))
    ws = jnp.where(mask[None], w_s, jnp.zeros_like(w_s))
    mixed = jnp.einsum('hij,bcjhd->bcihd', ws, vp) + b_s.T[None, None, :, :, None]
    return mixed.reshape(B, n_chunks * CHUNK, H, dh)[:, :L]

def mixer(h, pool_prefix, pos0, w_in, w_pool, pool_scale, sgu_ln_g, sgu_ln_b, sgu_w, sgu_b, w_out):
    B, L, _ = h.shape
    z = h @ w_in
    z_pool = z[..., :POOL_WIDTH]
    z_uv = jax.nn.gelu(z[..., POOL_WIDTH:], approximate=False)
    u = z_uv[..., :SGU_WIDTH].reshape(B, L, SGU_HEADS, SGU_HEAD_DIM)
    v = z_uv[..., SGU_WIDTH:].reshape(B, L, SGU_HEADS, SGU_HEAD_DIM)
    a_out, pool_buf = pool_mix(z_pool, pool_prefix, pos0, w_pool, pool_scale)
    v = head_layernorm(v, sgu_ln_g, sgu_ln_b)
    b_out = (u * sgu_mix(v, sgu_w, sgu_b)).reshape(B, L, SGU_WIDTH)
    mix = jnp.concatenate([a_out, b_out], axis=-1) @ w_out
    return mix, pool_buf, v.reshape(B, L, SGU_WIDTH)

def moe(h, w_router, b_router, w_up, b_up, w_down, b_down):
    B, L, D = h.shape
    T = B * L
    x = h.reshape(T, D)
    logits = (x @ w_router + b_router).astype(jnp.float32)
    top_logit, top_idx = lax.top_k(logits, TOP_K)
    top_w = jax.nn.softmax(top_logit, axis=-1).astype(x.dtype)
    A = T * TOP_K
    flat_e = top_idx.reshape(-1)
    flat_tok = jnp.arange(A) // TOP_K
    flat_w = top_w.reshape(-1)
    order = jnp.argsort(flat_e)
    sorted_e = flat_e[order]
    counts = jnp.bincount(flat_e, length=N_EXPERTS)
    padded = (counts + MOE_BLOCK - 1) // MOE_BLOCK * MOE_BLOCK
    pad_end = jnp.cumsum(padded)
    pad_start = pad_end - padded
    sort_start = jnp.cumsum(counts) - counts
    dest = pad_start[sorted_e] + (jnp.arange(A) - sort_start[sorted_e])
    n_blocks = -(-A // MOE_BLOCK) + N_EXPERTS
    n_slots = n_blocks * MOE_BLOCK
    slot_tok = jnp.full((n_slots,), T, dtype=jnp.int32).at[dest].set(flat_tok[order].astype(jnp.int32))
    slot_w = jnp.zeros((n_slots,), x.dtype).at[dest].set(flat_w[order])
    block_e = jnp.minimum(jnp.searchsorted(pad_end, jnp.arange(n_blocks) * MOE_BLOCK, side='right'),
                          N_EXPERTS - 1)
    x_pad = jnp.concatenate([x, jnp.zeros((1, D), x.dtype)], axis=0)
    xb = x_pad[slot_tok].reshape(n_blocks, MOE_BLOCK, D)

    def expert_block(args):
        xe, e = args
        gu = xe @ w_up[e] + b_up[e]
        glu = jnp.minimum(gu[:, :D_FF], SWIGLU_LIMIT)
        lin = jnp.clip(gu[:, D_FF:], -SWIGLU_LIMIT, SWIGLU_LIMIT)
        act = glu * jax.nn.sigmoid(SWIGLU_ALPHA * glu) * (lin + 1.0)
        return act @ w_down[e] + b_down[e]

    yb = lax.map(expert_block, (xb, block_e))
    y = jnp.zeros((T + 1, D), x.dtype).at[slot_tok].add(yb.reshape(n_slots, D) * slot_w[:, None])
    return y[:T].reshape(B, L, D)

def layer(x, p, pool_prefix, pos0, norm_mix, w_in, w_pool, pool_scale, sgu_ln_g, sgu_ln_b,
          sgu_w, sgu_b, w_out, norm_ffn, w_router, b_router, w_up, b_up, w_down, b_down,
          w_ple_gate, w_ple_proj):
    mix, pool_buf, v = mixer(rmsnorm(x, norm_mix), pool_prefix, pos0, w_in, w_pool, pool_scale,
                             sgu_ln_g, sgu_ln_b, sgu_w, sgu_b, w_out)
    x = x + mix
    x = x + moe(rmsnorm(x, norm_ffn), w_router, b_router, w_up, b_up, w_down, b_down)
    x = x + jax.nn.sigmoid(x @ w_ple_gate) * (p.astype(x.dtype) @ w_ple_proj)
    return x, pool_buf, v

def setup_inputs(seed: int = 0) -> dict:
    key = jax.random.key(seed)
    ks = jax.random.split(key, 32)
    f32 = jnp.float32
    nrm = lambda k, shape, scale: jax.random.normal(k, shape, f32) * scale
    return {
        "x_prompt": nrm(ks[0], (BATCH, SEQ, D_MODEL), 1.0),
        "x_sample": nrm(ks[1], (DEC_BATCH, DEC_SEQ, D_MODEL), 1.0),
        "state_pool": nrm(ks[2], (DEPTH, DEC_BATCH, POOL_BUF, POOL_WIDTH), 1.0),
        "p_prompt": nrm(ks[3], (DEPTH, BATCH, SEQ, PLE_DIM), 1.0),
        "p_sample": nrm(ks[4], (DEPTH, DEC_BATCH, DEC_SEQ, PLE_DIM), 1.0),
        "norm_mix": 1.0 + nrm(ks[5], (DEPTH, D_MODEL), 0.01),
        "w_in": nrm(ks[6], (DEPTH, D_MODEL, IN_WIDTH), D_MODEL ** -0.5),
        "w_pool": nrm(ks[7], (DEPTH, POOL_GROUPS, POOL_GROUP_DIM, POOL_GROUP_DIM), POOL_GROUP_DIM ** -0.5),
        "pool_scale": 1.0 + nrm(ks[8], (DEPTH, POOL_GROUPS, POOL_GROUP_DIM), 0.1),
        "sgu_ln_g": 1.0 + nrm(ks[9], (DEPTH, SGU_HEADS, SGU_HEAD_DIM), 0.01),
        "sgu_ln_b": nrm(ks[10], (DEPTH, SGU_HEADS, SGU_HEAD_DIM), 0.01),
        "sgu_w": nrm(ks[11], (DEPTH, SGU_HEADS, CHUNK, CHUNK), CHUNK ** -0.5),
        "sgu_b": 1.0 + nrm(ks[12], (DEPTH, SGU_HEADS, CHUNK), 0.1),
        "w_out": nrm(ks[13], (DEPTH, MIX_WIDTH, D_MODEL), MIX_WIDTH ** -0.5),
        "norm_ffn": 1.0 + nrm(ks[14], (DEPTH, D_MODEL), 0.01),
        "w_router": nrm(ks[15], (DEPTH, D_MODEL, N_EXPERTS), D_MODEL ** -0.5),
        "b_router": nrm(ks[16], (DEPTH, N_EXPERTS), 0.01),
        "w_up": nrm(ks[17], (DEPTH, N_EXPERTS, D_MODEL, 2 * D_FF), D_MODEL ** -0.5),
        "b_up": nrm(ks[18], (DEPTH, N_EXPERTS, 2 * D_FF), 0.01),
        "w_down": nrm(ks[19], (DEPTH, N_EXPERTS, D_FF, D_MODEL), D_FF ** -0.5),
        "b_down": nrm(ks[20], (DEPTH, N_EXPERTS, D_MODEL), 0.01),
        "w_ple_gate": nrm(ks[21], (DEPTH, D_MODEL, D_MODEL), D_MODEL ** -0.5),
        "w_ple_proj": nrm(ks[22], (DEPTH, PLE_DIM, D_MODEL), PLE_DIM ** -0.5),
        "norm_final": 1.0 + nrm(ks[23], (D_MODEL,), 0.01),
    }

def reference(x_prompt, x_sample, state_pool, p_prompt, p_sample, norm_mix, w_in, w_pool,
              pool_scale, sgu_ln_g, sgu_ln_b, sgu_w, sgu_b, w_out, norm_ffn, w_router, b_router,
              w_up, b_up, w_down, b_down, w_ple_gate, w_ple_proj, norm_final):
    xp, xs = x_prompt, x_sample
    zero_prefix = jnp.zeros((x_prompt.shape[0], POOL_BUF, POOL_WIDTH), x_prompt.dtype)
    pool_p, pool_s, v_s = [], [], []
    for i in range(DEPTH):
        lw = (norm_mix[i], w_in[i], w_pool[i], pool_scale[i], sgu_ln_g[i], sgu_ln_b[i], sgu_w[i],
              sgu_b[i], w_out[i], norm_ffn[i], w_router[i], b_router[i], w_up[i], b_up[i],
              w_down[i], b_down[i], w_ple_gate[i], w_ple_proj[i])
        xp, bp, _ = layer(xp, p_prompt[i], zero_prefix, 0, *lw)
        xs, bs, vs = layer(xs, p_sample[i], state_pool[i], PAST_LEN, *lw)
        pool_p.append(bp)
        pool_s.append(bs)
        v_s.append(vs)
    y_prompt = rmsnorm(xp, norm_final)
    y_sample = rmsnorm(xs, norm_final)
    new_pool_prompt = jnp.stack(pool_p, axis=0)
    new_pool_sample = jnp.stack(pool_s, axis=0)
    new_sgu_v_sample = jnp.stack(v_s, axis=0)
    return (y_prompt, y_sample, new_pool_prompt, new_pool_sample, new_sgu_v_sample)


_drawn_inputs = setup_inputs


def setup_inputs(seed=0):
    import zlib

    import numpy as np

    out = dict(_drawn_inputs(seed))
    spreads = {}
    factors = {'sgu_ln_g': 19.588,
     'sgu_ln_b': 65.024,
     'b_up': 8.0,
     'b_down': 59.875,
     'norm_final': 194.799,
     'norm_mix': 2.748,
     'norm_ffn': 10.959,
     'b_router': 8.0}
    for name, (base, spread) in spreads.items():
        noise = np.random.default_rng([zlib.crc32(name.encode()), seed]).standard_normal(out[name].shape)
        drawn = base * np.exp(spread * noise) if base else spread * noise
        out[name] = __import__('jax').numpy.asarray(drawn.astype(out[name].dtype))
    for name, factor in factors.items():
        out[name] = (out[name] * factor).astype(out[name].dtype)
    return out
```

```python
from contextlib import ExitStack

import concourse.bass as bass
from concourse import mybir

F32 = mybir.dt.float32
F32R = mybir.dt.float32r
I32 = mybir.dt.int32
U32 = mybir.dt.uint32
ALU = mybir.AluOpType
ACT = mybir.ActivationFunctionType
AX = mybir.AxisListType

P = 128
RING = 6
SPLIT = 3
UP_CHUNKS = 8
DN_CHUNKS = 4
STEP_CHUNKS = UP_CHUNKS + DN_CHUNKS
POOL_LO = (4, 10)
NO_ROW = 4096


def build(nc, x_prompt, x_sample, state_pool, p_prompt, p_sample, norm_mix, w_in, w_pool, pool_scale,
          sgu_ln_g, sgu_ln_b, sgu_w, sgu_b, w_out, norm_ffn, w_router, b_router, w_up, b_up, w_down,
          b_down, w_ple_gate, w_ple_proj, norm_final,
          y_prompt, y_sample, new_pool_prompt, new_pool_sample, new_sgu_v):
    SEQ, D = x_prompt.shape[1:]
    DB, DS = x_sample.shape[:2]
    NS = DB * DS
    T = SEQ + NS
    TT = SEQ // P + 1
    LAST = TT - 1
    NT = [P] * LAST + [NS]
    PW = state_pool.shape[3]
    PB = state_pool.shape[2]
    G = PW // P
    WINDOWS = (2, 4, 8, 16)
    KD = D // P
    IN = w_in.shape[2]
    SG = (IN - PW) // 2
    E = w_router.shape[2]
    FF = w_down.shape[2]
    TOPK = 4
    PD = w_ple_proj.shape[1]
    KP = PD // P
    OVER = T * TOPK // P - 1
    NBLK = E + OVER + 2
    LEAD = 16
    SB = LEAD + DS
    EXT = LEAD + SEQ + DB * SB
    NORM_EPS, LN_EPS = 1e-6, 1e-5
    LIMIT, ALPHA = 7.0, 1.702

    xn_dram = nc.dram_tensor("xn_rows", [T, D], F32, kind="Internal").ap()
    y4_dram = nc.dram_tensor("expert_rows", [T * TOPK, D], F32, kind="Internal").ap()
    up_dram = w_up.rearrange("a e (c p) n -> (a e c) p n", p=P)
    dn_dram = w_down.rearrange("a e (c j p) n -> (a e c) p j n", p=P, j=2)

    ctx = ExitStack()
    with ctx:
        def sb(name, shape, dt=F32, scope=ctx):
            return scope.enter_context(nc.sbuf_tensor(name, shape, dt))

        def sem(name):
            return ctx.enter_context(nc.semaphore(name))

        ident = sb("ident", [P, P])
        resid = sb("resid", [P, TT, D])
        topw = sb("topw", [P, TT, TOPK])
        block_of = sb("block_of", [P, TT, E])
        pos_row = sb("pos_row", [P, 2, TT, E])
        slot1 = sb("slot1", [P, P])
        block_iota = sb("block_iota", [P, NBLK])
        block_expert = sb("block_expert", [P, NBLK])
        block_expert_i = sb("block_expert_i", [P, NBLK], I32)
        over_i = sb("over_i", [P, 1], I32)
        cur_block = sb("cur_block", [P, 1])
        cur_expert = sb("cur_expert", [P, 1])
        bias_row = sb("bias_row", [P, 1])
        bias_hl = sb("bias_hl", [P, 2 * FF + D], F32R)
        half_neg = sb("half_neg", [P, 16])
        with ExitStack() as s:
            actsT = sb("actsT", [P, KD, TT * P], scope=s)
        ple = sb("ple", [P, TT, D])
        with ExitStack() as s:
            w_in_sb = sb("w_in_sb", [P, KD, IN], scope=s)
        with ExitStack() as s:
            w_out_sb = sb("w_out_sb", [P, KD, D], scope=s)
        raw = sb("raw", [P, RING, 2 * FF])

        with ExitStack() as s:
            with ExitStack() as s2:
                ext = sb("ext", [P, G, EXT], scope=s2)
                uT = sb("uT", [P, G, T], scope=s2)
            w_proj_sb = sb("w_proj_sb", [P, KP, D], scope=s)
            p_sb = sb("p_sb", [P, TT, PD], scope=s)
            pT = sb("pT", [P, KP, TT * P], scope=s)
            sb("pad0", [P, 512], scope=s)
            gain = sb("gain", [P, D], scope=s)
            gain2 = sb("gain2", [P, D], scope=s)
            xn = sb("xn", [P, 2, D], scope=s)
            h2T = sb("h2T", [P, 2, KD, P], scope=s)
            junk = sb("junk", [P, D], scope=s)
            with ExitStack() as s2:
                v_sb = sb("v_sb", [P, TT, SG], scope=s2)
                sumA = sb("sumA", [P, EXT], scope=s2)
                sumB = sb("sumB", [P, EXT], scope=s2)
                diff = sb("diff", [P, T], scope=s2)
                gated = sb("gated", [P, SG], scope=s2)
            bias_raw = sb("bias_raw", [P, 2 * FF + D], scope=s)
            sb("pad1", [P, 2048], scope=s)
            w_pool_sb = sb("w_pool_sb", [P, G, P], scope=s)
            sgu_w_sb = sb("sgu_w_sb", [P, G, P], scope=s)
            wsT = sb("wsT", [P, G, P], scope=s)
            sgu_bias = sb("sgu_bias", [P, G, P], scope=s)
            ln_g = sb("ln_g", [P, SG], scope=s)
            ln_b = sb("ln_b", [P, SG], scope=s)
            state_sb = sb("state_sb", [P, PW], scope=s)
            scale4 = sb("scale4", [G, P], scope=s)
            scaleT = sb("scaleT", [P, G], scope=s)
            same_seq = sb("same_seq", [P, DB, DS], scope=s)
            block_w = sb("block_w", [P, G, NS], scope=s)
            rep = sb("rep", [P, NS], scope=s)
            head_fix = sb("head_fix", [P, G, LEAD], scope=s)
            new_cols = sb("new_cols", [P, G, NS], scope=s)
            pos_iota = sb("pos_iota", [P, LEAD], scope=s)
            pool_rows = sb("pool_rows", [P, PW], scope=s)
            pool_rows_s = sb("pool_rows_s", [P, PW], scope=s)
            stats = sb("stats", [P, G, 6], scope=s)
            mean_var = sb("mean_var", [P, TT, G, 2], scope=s)
            ln_var = sb("ln_var", [P, TT, G], scope=s)
            ln_rstd = sb("ln_rstd", [P, TT, G], scope=s)
            sq1 = sb("sq1", [P, TT], scope=s)
            var1 = sb("var1", [P, TT], scope=s)
            rstd1 = sb("rstd1", [P, TT], scope=s)
            sq2 = sb("sq2", [P, TT], scope=s)
            var2 = sb("var2", [P, TT], scope=s)
            rstd2 = sb("rstd2", [P, TT], scope=s)
            w_router_sb = sb("w_router_sb", [P, KD, E], scope=s)
            b_router_sb = sb("b_router_sb", [1, E], scope=s)
            ones = sb("ones", [P, P], scope=s)
            before = sb("before", [P, P], scope=s)
            logits = sb("logits", [P, TT, E], scope=s)
            top8 = sb("top8", [P, TT, 8], scope=s)
            top_i = sb("top_i", [P, TT, 8], U32, scope=s)
            top_f = sb("top_f", [P, TT, TOPK], scope=s)
            neg_max = sb("neg_max", [P, TT], scope=s)
            exps = sb("exps", [P, TT, TOPK], scope=s)
            exp_sum = sb("exp_sum", [P, TT], scope=s)
            exp_rcp = sb("exp_rcp", [P, TT], scope=s)
            expert_iota = sb("expert_iota", [P, E], scope=s)
            chosen = sb("chosen", [P, TT, TOPK, E], scope=s)
            chosen_row = sb("chosen_row", [P, TT, TOPK, E], scope=s)
            row_code = sb("row_code", [P, TT, TOPK], scope=s)
            mask = sb("mask", [P, TT, E], scope=s)
            rank = sb("rank", [P, TT, E], scope=s)
            depth = sb("depth", [P, TT, E], scope=s)
            first = sb("first", [P, TT, E], scope=s)
            count = sb("count", [P, E], scope=s)
            over = sb("over", [P, E], scope=s)
            over_end = sb("over_end", [P, E], scope=s)
            over_from = sb("over_from", [P, E], scope=s)
            over_cmp = sb("over_cmp", [P, OVER + 2, E], scope=s)

        with ExitStack() as s:
            w_hi = sb("w_hi", [P, SPLIT, 2 * FF], F32R, scope=s)
            w_lo = sb("w_lo", [P, SPLIT, 2 * FF], F32R, scope=s)
            x_rows = sb("x_rows", [P, D], scope=s)
            xT_hi = sb("xT_hi", [P, KD, P], F32R, scope=s)
            xT_lo = sb("xT_lo", [P, KD, P], F32R, scope=s)
            glu = sb("glu", [P, FF], scope=s)
            sig = sb("sig", [P, FF], scope=s)
            lin = sb("lin", [P, FF], scope=s)
            aT_hi = sb("aT_hi", [P, KD, P], F32R, scope=s)
            aT_lo = sb("aT_lo", [P, KD, P], F32R, scope=s)
            y_rows = sb("y_rows", [P, D], scope=s)
            picks = sb("picks", [P, TT, P], scope=s)
            same_block = sb("same_block", [P, TT, E], scope=s)
            in_block = sb("in_block", [P, 2, TT, E], scope=s)
            tok_slot = sb("tok_slot", [P, 2, TT], scope=s)
            junk_b = sb("junk_b", [P, NBLK], scope=s)
            rows = sb("rows", [P, 4], U32, scope=s)
            rows_tmp = sb("rows_tmp", [P, 3], U32, scope=s)
            token_of = sb("token_of", [P, 1], U32, scope=s)
            oh_up = sb("oh_up", [P, P], F32R, scope=s)
            oh_dn = sb("oh_dn", [P, P], F32R, scope=s)

        with ExitStack() as s:
            gate_w = sb("gate_w", [P, KD, D], scope=s)
            x2T = sb("x2T", [P, 2, KD, P], scope=s)
            gate = sb("gate", [P, 2, D], scope=s)
            out_rows = sb("out_rows", [P, 2, D], scope=s)
            gain_f = sb("gain_f", [P, D], scope=s)
            junk_t = sb("junk_t", [P, D], scope=s)
            sq3 = sb("sq3", [P, TT], scope=s)
            var3 = sb("var3", [P, TT], scope=s)
            rstd3 = sb("rstd3", [P, TT], scope=s)
        STORES = 3 + DB
        YB = 3

        ps = ctx.enter_context(nc.psum_tensor("ps", [P, 8, 512], F32))

        JOBS = [(("xT", t), "A") for t in range(TT)] + [(("misc", 0), "V"), (("blockw", 0), "V")]
        JOBS += [(("v", t), "A") for t in range(TT)]
        JOBS += [(("z", m), "A") for m in range(2 * G)] + [(("newpool", 0), "A")]
        JOBS += [(("pool", g), "V") for g in range(G)]
        JOBS += [(("gating", t), "V") for t in range(TT)]
        for t in range(TT + 2):
            if t < TT:
                JOBS.append((("out", t), "V"))
            if 0 <= t - 1 < TT:
                JOBS.append((("h2T", t - 1), "A"))
            if 0 <= t - 2 < TT:
                JOBS.append((("logits", t - 2), "V"))
        JOBS += [(("rank", 0), "V")] + [(("pT", t), "A") for t in range(TT)] + [(("ple", t), "A") for t in range(TT)]
        JOB = {name: n for n, (name, _) in enumerate(JOBS)}
        EMPTIED = {}
        for n, (name, who) in enumerate(JOBS):
            EMPTIED[name] = sum(w == who for _, w in JOBS[:n + 1])
        TOTAL = {who: sum(w == who for _, w in JOBS) for who in "AV"}

        s_job = sem("job_filled")
        s_emptied = {"A": sem("job_emptied_act"), "V": sem("job_emptied_dve")}

        def bank(name, b=0):
            return ps[:, 2 * (JOB[name] % 4) + b, :]

        def banks(name):
            n = 2 * (JOB[name] % 4)
            return ps[:, n:n + 2, :]

        def job_free(pe, name):
            n = JOB[name]
            if n >= 4:
                old, who = JOBS[n - 4]
                pe.wait_ge(s_emptied[who], EMPTIED[old])

        def job_filled(eng, name):
            eng.wait_ge(s_job, JOB[name] + 1)

        ld = {n: sem("ld_" + n) for n in (
            "x gain w_in_v w_in_z small pool_w state sgu ln w_out gain2 router bias ple p gate gain_f".split())}
        s_ident = sem("ident_made")
        s_const = sem("constants_made")
        s_resid0 = sem("resid_tail_zeroed")
        s_sq = sem("squares_summed")
        s_var = sem("variances")
        s_rstd = sem("rstds")
        s_xn = sem("xn_ready")
        s_chain = sem("dve_chain")
        s_achain = sem("act_chain")
        s_pchain = sem("pool_chain")
        s_wpart = sem("mask_parts")
        s_lnv = sem("ln_variances")
        s_lnr = sem("ln_rstds")
        s_v = sem("v_normed")
        s_ext0 = sem("ext_zeroed")
        s_sum = sem("window_sums")
        s_diff = sem("diffs")
        s_mix = sem("mix_written")
        s_pad = sem("mix_padded")
        s_xrow = [sem(f"xn_rows_stored_{t}") for t in range(TT)]
        s_top = sem("tops")
        s_exp = sem("exps")
        s_mask = sem("masks")
        s_route = sem("routing_ready")
        s_bias = sem("bias_split")
        s_out = sem("outputs_stored")
        s_p0 = sem("p_tail_zeroed")

        ring = [sem(f"raw_landed_{i}") for i in range(RING)]
        s_hi = sem("chunk_hi")
        s_lo = {"V": sem("chunk_lo_dve"), "P": sem("chunk_lo_pool")}
        s_chunk = sem("chunk_used")
        s_picks = sem("picks_ready")
        s_rowps = sem("slots_summed")
        s_rows = sem("row_numbers")
        s_gather = sem("x_rows_landed")
        s_xtp = sem("x_transposed")
        s_xhi = sem("xT_hi_ready")
        s_xlo = sem("xT_lo_ready")
        s_oh = sem("bias_picks_ready")
        s_glu = sem("glu_ready")
        s_lin = sem("lin_ready")
        s_sig = sem("sigmoid_ready")
        s_gs = sem("swish_ready")
        s_act = sem("activation_ready")
        s_atp = sem("activation_transposed")
        s_ahi = sem("aT_hi_ready")
        s_alo = sem("aT_lo_ready")
        s_y = sem("y_rows_ready")
        s_scat = sem("y_rows_stored")
        s_moe = sem("moe_chain")

        s_yk = [sem(f"expert_rows_landed_{i}") for i in range(YB)]
        s_comb = sem("moe_added")
        s_x2tp = sem("x2_transposed")
        s_x2T = sem("x2T_ready")
        s_gmm = sem("gate_done")
        s_gate = sem("gate_sigmoid")
        s_x3 = sem("x3_ready")
        s_sq3 = sem("squares3")
        s_var3 = sem("var3_ready")
        s_rstd3 = sem("rstd3_ready")
        s_orow = sem("out_rows_ready")
        s_ost = [sem("out_rows_stored_even"), sem("out_rows_stored_odd")]
        s_tchain = sem("tail_chain")

        gu = ps[:, 0:4, :].rearrange("p a b -> p (a b)")
        dn = ps[:, 4:6, :].rearrange("p a b -> p (a b)")
        tp = ps[:, 6:8, :].rearrange("p a b -> p (a b)")
        slot_sum = ps[:, 4, 0:1]
        LOS = {"V": [sum(c % STEP_CHUNKS not in POOL_LO for c in range(s)) for s in range(2 * STEP_CHUNKS + 1)],
               "P": [sum(c % STEP_CHUNKS in POOL_LO for c in range(s)) for s in range(2 * STEP_CHUNKS + 1)]}
        PER = {"V": STEP_CHUNKS - len(POOL_LO), "P": len(POOL_LO)}

        def lo_by(s):
            return "P" if s % STEP_CHUNKS in POOL_LO else "V"

        def wait_lo(eng, J, s):
            who = lo_by(s)
            eng.wait_ge(s_lo[who], PER[who] * J + LOS[who][s] + 1)

        def wait_hi(eng, J, s):
            eng.wait_ge(s_hi, STEP_CHUNKS * J + s + 1)

        def wait_landed(eng, J, s):
            eng.wait_ge(ring[s % RING], 32 * J + 16 * (s // RING) + 16)

        def tail_gate(act, t):
            act.wait_ge(s_gmm, t + 1)
            if t >= 2:
                act.wait_ge(s_x3, t - 1)
            act.activation(gate[:, t % 2, :], ps[:, 2 * (t % 2):2 * (t % 2) + 2, :].rearrange("p a n -> p (a n)"),
                           ACT.Sigmoid).then_inc(s_gate, 1)
            act.wait_ge(s_x3, t + 1)
            if t >= 1:
                act.wait_ge(s_sq3, t)
            act.activation(junk_t[:], resid[:, t, :], ACT.Square, accum_out=sq3[:, t:t + 1]).then_inc(s_sq3, 1)

        def gate_product(pe, t):
            pe.wait_ge(s_x2T, t + 1)
            pe.wait_ge(ld["gate"], 32)
            if t >= 2:
                pe.wait_ge(s_gate, t - 1)
            for k in range(KD):
                for b in range(2):
                    mm = pe.matmul(ps[:, 2 * (t % 2) + b, :], x2T[:, t % 2, k, :], gate_w[:, k, b * 512:(b + 1) * 512],
                                   start=(k == 0), stop=(k == KD - 1))
            mm.then_inc(s_gmm, 1)

        block = ctx.enter_context(nc.Block())

        @block.sync
        def _(sp):
            for t in range(LAST):
                sp.dma_start(resid[:, t, :], x_prompt[0, t * P:(t + 1) * P, :]).then_inc(ld["x"], 16)
            sp.wait_ge(s_resid0, 1)
            sp.dma_start(resid[0:NS, LAST, :], x_sample.rearrange("b s d -> (b s) d")).then_inc(ld["x"], 16)
            w_in_v = w_in.rearrange("a (k p) n -> p (a k) n", p=P)
            for k in range(0, KD, 2):
                sp.dma_start(w_in_sb[:, k:k + 2, PW + SG:], w_in_v[:, k:k + 2, PW + SG:]).then_inc(ld["w_in_v"], 16)
            for k in range(0, KD, 2):
                sp.dma_start(w_in_sb[:, k:k + 2, 0:PW + SG], w_in_v[:, k:k + 2, 0:PW + SG]).then_inc(ld["w_in_z"], 16)
            sp.wait_ge(s_job, JOB[("z", 2 * G - 1)] + 1)
            sp.dma_start(w_out_sb[:], w_out.rearrange("a (k p) n -> p (a k) n", p=P)).then_inc(ld["w_out"], 16)
            for t in range(TT):
                sp.wait_ge(s_xn, TT + t + 1)
                sp.dma_start(xn_dram[t * P:t * P + NT[t], :], xn[0:NT[t], t % 2, :]).then_inc(s_xrow[t], 16)
            sp.wait_ge(s_job, JOB[("out", LAST)] + 1)

            def raw_free(J, s):
                if isinstance(J, int):
                    if STEP_CHUNKS * J + s >= RING:
                        wait_hi(sp, J, s - RING)
                        wait_lo(sp, J, s - RING)
                    return
                who = lo_by(s - RING)
                hi = sp.to_reg(J * STEP_CHUNKS + (s - RING + 1))
                lo = sp.to_reg(J * PER[who] + (LOS[who][s - RING] + 1))
                sp.wait_ge(s_job, JOB[("out", LAST)] + 1)
                sp.wait_ge(s_hi, hi)
                sp.wait_ge(s_lo[who], lo)

            def load_up(J, s, e, c):
                raw_free(J, s)
                sp.dma_start(raw[:, s % RING, :], up_dram[bass.ds(e * UP_CHUNKS + c, 1), :, :].rearrange(
                    "a p n -> p (a n)")).then_inc(ring[s % RING], 16)

            def load_dn(J, s, e, c):
                raw_free(J, s)
                sp.dma_start(raw[:, s % RING, :].rearrange("p (j n) -> p j n", j=2),
                             dn_dram[bass.ds(e * DN_CHUNKS + c, 1), :, :, :].rearrange(
                                 "a p j n -> p (a j) n")).then_inc(ring[s % RING], 16)

            def step(J, e_up, e_dn):
                for c in range(UP_CHUNKS):
                    load_up(J, UP_CHUNKS + c, e_up, c)
                for c in range(DN_CHUNKS):
                    load_dn(J, 2 * UP_CHUNKS + c, e_dn, c)

            for c in range(UP_CHUNKS):
                load_up(0, c, 0, c)
            with sp.Fori(0, E - 1) as J:
                step(J, J + 1, J)
            sp.wait_ge(s_route, 1)
            n_over = sp.value_load(over_i[0:1, 0:1], min_val=0, max_val=OVER)
            with sp.Fori(0, OVER) as b:
                with sp.If(b < n_over):
                    e_up = sp.value_load(block_expert_i[0:1, bass.ds(b + E, 1)], min_val=0, max_val=E - 1)
                    e_dn = sp.value_load(block_expert_i[0:1, bass.ds(b + (E - 1), 1)], min_val=0, max_val=E - 1)
                    step(b + (E - 1), e_up, e_dn)
            e_dn = sp.value_load(block_expert_i[0:1, bass.ds(n_over + (E - 1), 1)], min_val=0, max_val=E - 1)
            for c in range(DN_CHUNKS):
                load_dn(n_over + (E - 1), UP_CHUNKS + c, e_dn, c)
            sp.wait_ge(s_y, n_over + E)
            sp.dma_start(gain_f[:], norm_final.partition_broadcast(P)).then_inc(ld["gain_f"], 16)
            gate_v = w_ple_gate.rearrange("a (k p) n -> p (a k) n", p=P)
            sp.dma_start(gate_w[:, 0:KD // 2, :], gate_v[:, 0:KD // 2, :]).then_inc(ld["gate"], 16)
            sp.dma_start(gate_w[:, KD // 2:, :], gate_v[:, KD // 2:, :]).then_inc(ld["gate"], 16)
            sp.wait_ge(s_scat, 16 * n_over + 16 * E)
            y4 = y4_dram.rearrange("(t k) d -> t (k d)", k=TOPK)
            for t in range(TT):
                if t >= YB:
                    sp.wait_ge(s_comb, t - YB + 1)
                sp.dma_start(raw[0:NT[t], 2 * (t % YB):2 * (t % YB) + 2, :].rearrange("p a n -> p (a n)"),
                             y4[t * P:t * P + NT[t], :]).then_inc(s_yk[t % YB], 16)
            for t in range(TT):
                sp.wait_ge(s_orow, t + 1)
                dst = y_prompt[0, t * P:(t + 1) * P, :] if t < LAST else y_sample.rearrange("b s d -> (b s) d")
                sp.dma_start(dst, out_rows[0:NT[t], t % 2, :]).then_inc(s_ost[t % 2], 16)
            sp.wait_ge(s_ost[0], 16 * ((TT + 1) // 2))
            sp.wait_ge(s_ost[1], 16 * (TT // 2))
            sp.wait_ge(s_out, 16 * STORES)

        @block.gpsimd
        def _(pool):
            chain = [0]

            def link(ins):
                chain[0] += 1
                ins.then_inc(s_pchain, 1)
                pool.wait_ge(s_pchain, chain[0])

            pool.memset(resid[:, LAST, :], 0.0).then_inc(s_resid0, 1)
            pool.memset(half_neg[:], -0.5).then_inc(s_const, 1)
            link(pool.memset(ident[:], 0.0))
            pool.affine_select(out=ident[:], in_=ident[:], compare_op=ALU.not_equal, fill=1.0, base=0,
                               pattern=[[-1, P]], channel_multiplier=1).then_inc(s_ident, 1)
            pool.wait_ge(s_const, 1)
            for t in range(TT):
                pool.wait_ge(s_var, t + 1)
                pool.tensor_tensor(rstd1[:, t:t + 1], var1[:, t:t + 1], half_neg[:, 0:1], ALU.pow).then_inc(s_rstd, 1)
            pool.wait_ge(ld["sgu"], 16)
            pool.affine_select(out=sgu_w_sb[:], in_=sgu_w_sb[:], compare_op=ALU.is_ge, fill=0.0, base=0,
                               pattern=[[0, G], [-1, P]], channel_multiplier=1).then_inc(s_wpart, 1)
            link(pool.memset(same_seq[:], 1.0))
            link(pool.affine_select(out=same_seq[:], in_=same_seq[:], compare_op=ALU.is_ge, fill=0.0, base=0,
                                    pattern=[[-DS, DB], [0, DS]], channel_multiplier=1))
            pool.affine_select(out=same_seq[:], in_=same_seq[:], compare_op=ALU.is_ge, fill=0.0, base=DS - 1,
                               pattern=[[DS, DB], [0, DS]], channel_multiplier=-1).then_inc(s_wpart, 1)
            pool.memset(ext[:, :, 0:LEAD], 0.0).then_inc(s_ext0, 1)
            pool.memset(ext[:, :, LEAD + SEQ:], 0.0).then_inc(s_ext0, 1)
            link(pool.iota(pos_iota[:], pattern=[[1, LEAD]], base=1, channel_multiplier=0,
                           allow_small_or_imprecise_dtypes=True))
            for g, w in enumerate(WINDOWS):
                pool.tensor_scalar(head_fix[:, g, :], pos_iota[:], float(w), None, ALU.min).then_inc(s_const, 1)
            pool.memset(ones[:], 1.0).then_inc(s_const, 1)
            link(pool.memset(before[:], 1.0))
            pool.affine_select(out=before[:], in_=before[:], compare_op=ALU.is_gt, fill=0.0, base=0,
                               pattern=[[1, P]], channel_multiplier=-1).then_inc(s_const, 1)
            pool.iota(expert_iota[:], pattern=[[1, E]], base=0, channel_multiplier=0,
                      allow_small_or_imprecise_dtypes=True).then_inc(s_const, 1)
            pool.iota(slot1[:], pattern=[[1, P]], base=1, channel_multiplier=0,
                      allow_small_or_imprecise_dtypes=True).then_inc(s_const, 1)
            pool.iota(block_iota[:], pattern=[[1, NBLK]], base=0, channel_multiplier=0,
                      allow_small_or_imprecise_dtypes=True).then_inc(s_const, 1)
            pool.iota(row_code[:], pattern=[[TOPK * P, TT], [1, TOPK]], base=-NO_ROW, channel_multiplier=TOPK,
                      allow_small_or_imprecise_dtypes=True).then_inc(s_const, 1)
            pool.memset(mask[:], 0.0).then_inc(s_const, 1)
            pool.memset(cur_block[:], 0.0).then_inc(s_const, 1)
            link(pool.iota(bias_row[:], pattern=[[0, 1]], base=0, channel_multiplier=1,
                           allow_small_or_imprecise_dtypes=True))
            link(pool.tensor_scalar(bias_row[E:2 * E, :], bias_row[E:2 * E, :], float(E), None, ALU.subtract))
            pool.tensor_scalar(bias_row[2 * E:P, :], bias_row[2 * E:P, :], 1000.0, None, ALU.add).then_inc(s_const, 1)
            pool.wait_ge(s_ext0, 2)
            pool.wait_ge(s_const, 14)
            for g in range(G):
                job_emptied = EMPTIED[("z", g)]
                pool.wait_ge(s_emptied["A"], job_emptied)
                pool.wait_ge(s_emptied["V"], EMPTIED[("misc", 0)])
                src = ext[:, g, :]
                if g >= 1:
                    pool.wait_ge(s_diff, g)
                for i in range(g + 1):
                    dst = (sumA, sumB)[(g - i) % 2]
                    sh = 1 << i
                    lo = (2 << i) - 1
                    ins = pool.tensor_tensor(dst[:, lo:EXT], src[:, lo:EXT], src[:, lo - sh:EXT - sh], ALU.add)
                    if i < g:
                        link(ins)
                    else:
                        ins.then_inc(s_sum, 1)
                    src = dst
            for t in range(TT):
                pool.wait_ge(s_lnv, t + 1)
                pool.tensor_tensor(ln_rstd[0:NT[t], t, :], ln_var[0:NT[t], t, :], half_neg[0:NT[t], 0:G],
                                   ALU.pow).then_inc(s_lnr, 1)
            pool.wait_ge(s_lnr, TT)
            for t in range(TT):
                pool.wait_ge(s_var, TT + t + 1)
                pool.tensor_tensor(rstd2[:, t:t + 1], var2[:, t:t + 1], half_neg[:, 0:1], ALU.pow).then_inc(s_rstd, 1)
            pool.wait_ge(s_route, 1)
            for t in range(TT):
                pool.wait_ge(s_xrow[t], 16)
            pool.wait_ge(s_out, 16 * STORES)
            pool.wait_ge(s_emptied["A"], TOTAL["A"])
            pool.memset(x_rows[:], 0.0).then_inc(s_moe, 1)
            pool.wait_ge(s_moe, 1)

            last_token = pool.to_reg(T - 1)
            last_row = pool.to_reg(T * TOPK - 1)

            def gather(u):
                found, used = (u + 1, u) if isinstance(u, int) else (pool.to_reg(u + 1), pool.to_reg(u))
                pool.wait_ge(s_moe, 1)
                pool.wait_ge(s_rows, found)
                if not (isinstance(u, int) and u == 0):
                    pool.wait_ge(s_xtp, used)
                pool.indirect_dma_start(x_rows[:], None, xn_dram[:, :],
                                        bass.IndirectOffsetOnAxis(ap=token_of[:, 0:1], axis=0),
                                        bounds_check=last_token, oob_is_err=False).then_inc(s_gather, 16)

            def scatter(u, col):
                ready = u + 1 if isinstance(u, int) else pool.to_reg(u + 1)
                pool.wait_ge(s_moe, 1)
                pool.wait_ge(s_y, ready)
                pool.indirect_dma_start(y4_dram[:, :], bass.IndirectOffsetOnAxis(ap=rows[:, col:col + 1], axis=0),
                                        y_rows[:], None,
                                        bounds_check=last_row, oob_is_err=False).then_inc(s_scat, 16)

            def lo_part(J, s):
                wait_hi(pool, J, s)
                pool.tensor_tensor(w_lo[:, s % SPLIT, :], raw[:, s % RING, :], w_hi[:, s % SPLIT, :].bitcast(F32),
                                   ALU.subtract).then_inc(s_lo["P"], 1)

            def swish(u):
                pool.wait_ge(s_sig, u + 1)
                pool.tensor_tensor(sig[:], glu[:], sig[:], ALU.mult).then_inc(s_gs, 1)

            def step(J, scatters=True):
                for x in range(STEP_CHUNKS):
                    s = UP_CHUNKS + x
                    if x == 7:
                        gather(J + 2)
                        if scatters:
                            scatter(J - 1, 3)
                    if lo_by(s) == "P":
                        lo_part(J, s)
                swish(J + 1)

            gather(0)
            for s in range(UP_CHUNKS):
                if lo_by(s) == "P":
                    lo_part(0, s)
            gather(1)
            swish(0)
            step(0, scatters=False)
            step(1)
            with pool.Fori(2, E - 1) as J:
                step(J)
            n_over = pool.value_load(over_i[0:1, 0:1], min_val=0, max_val=OVER)
            with pool.Fori(0, OVER) as b:
                with pool.If(b < n_over):
                    step(b + (E - 1))
            for x in range(DN_CHUNKS):
                if lo_by(UP_CHUNKS + x) == "P":
                    lo_part(n_over + (E - 1), UP_CHUNKS + x)
            scatter(n_over + (E - 2), 2)
            scatter(n_over + (E - 1), 1)
            for t in range(TT):
                pool.wait_ge(s_var3, t + 1)
                pool.tensor_tensor(rstd3[:, t:t + 1], var3[:, t:t + 1], half_neg[:, 0:1], ALU.pow).then_inc(s_rstd3, 1)

        @block.scalar
        def _(act):
            act.dma_start(gain[:], norm_mix[0].partition_broadcast(P)).then_inc(ld["gain"], 16)
            act.dma_start(sgu_w_sb[:], sgu_w[0].rearrange("h i j -> i h j")).then_inc(ld["sgu"], 16)
            act.dma_start(state_sb[0:DB * PB, :], state_pool[0].rearrange("b r c -> (b r) c")).then_inc(ld["state"], 16)
            act.dma_start(scale4[:], pool_scale[0]).then_inc(ld["state"], 16)
            act.dma_start(w_pool_sb[:], w_pool[0].rearrange("g c d -> c g d")).then_inc(ld["pool_w"], 16)
            act.dma_start(sgu_bias[:].rearrange("p h i -> p (h i)"),
                          sgu_b.rearrange("a h i -> (a h i)").partition_broadcast(P)).then_inc(ld["small"], 16)
            act.dma_start(ln_g[:], sgu_ln_g.rearrange("a h i -> (a h i)").partition_broadcast(P)).then_inc(ld["ln"], 16)
            act.dma_start(ln_b[:], sgu_ln_b.rearrange("a h i -> (a h i)").partition_broadcast(P)).then_inc(ld["ln"], 16)
            act.dma_start(gain2[:], norm_ffn[0].partition_broadcast(P)).then_inc(ld["gain2"], 16)
            act.dma_start(w_router_sb[:], w_router[0].rearrange("(k p) e -> p k e", p=P)).then_inc(ld["router"], 16)
            act.dma_start(b_router_sb[:], b_router).then_inc(ld["router"], 16)
            act.dma_start(new_pool_sample[0, :, 0:PB - DS, :], state_pool[0, :, DS:PB, :]).then_inc(s_out, 16)

            for t in range(TT):
                act.wait_ge(ld["x"], 16 * TT)
                if t >= 1:
                    act.wait_ge(s_sq, t)
                act.activation(junk[:], resid[:, t, :], ACT.Square, accum_out=sq1[:, t:t + 1]).then_inc(s_sq, 1)
            for t in range(TT):
                job_filled(act, ("xT", t))
                act.activation(actsT[:, :, t * P:(t + 1) * P], banks(("xT", t)).rearrange("p a (b n) -> p (a b) n", n=P),
                               ACT.Copy).then_inc(s_emptied["A"], 1)
            for t in range(TT):
                n = NT[t]
                job_filled(act, ("v", t))
                act.activation(v_sb[0:n, t, :], bank(("v", t))[0:n, :], ACT.Gelu).then_inc(s_emptied["A"], 1)
            act.wait_ge(s_ext0, 2)
            act.wait_ge(s_emptied["V"], EMPTIED[("misc", 0)])
            for m in range(2 * G):
                name = ("z", m)
                job_filled(act, name)
                new = bank(name, 1)[:, 0:NS]
                if m < G:
                    act.activation(ext[:, m, LEAD:LEAD + SEQ], bank(name), ACT.Copy)
                    act.activation(new_cols[:, m, :], new, ACT.Copy)
                    act.activation(ext[:, m, LEAD + SEQ:].rearrange("p (b s) -> p b s", b=DB)[:, :, LEAD:],
                                   new.rearrange("p (b s) -> p b s", b=DB), ACT.Copy).then_inc(s_emptied["A"], 1)
                else:
                    act.activation(uT[:, m - G, 0:SEQ], bank(name), ACT.Gelu)
                    act.activation(uT[:, m - G, SEQ:], new, ACT.Gelu).then_inc(s_emptied["A"], 1)
            job_filled(act, ("newpool", 0))
            act.activation(pool_rows[0:PB, :], bank(("newpool", 0))[0:PB, :], ACT.Copy).then_inc(s_achain, 1)
            act.activation(pool_rows_s[0:NS, :], bank(("newpool", 0), 1)[0:NS, :], ACT.Copy).then_inc(s_emptied["A"], 1)
            act.wait_ge(s_achain, 1)
            act.dma_start(new_pool_prompt[0, 0], pool_rows[0:PB, :]).then_inc(s_out, 16)
            act.wait_ge(s_emptied["A"], EMPTIED[("newpool", 0)])
            for b in range(DB):
                act.dma_start(new_pool_sample[0, b, PB - DS:PB, :], pool_rows_s[b * DS:(b + 1) * DS, :]).then_inc(s_out, 16)
            act.wait_ge(s_v, TT)
            act.dma_start(new_sgu_v.rearrange("a b s c -> (a b s) c"), v_sb[0:NS, LAST, :]).then_inc(s_out, 16)
            act.wait_ge(s_mix, G + TT)
            act.wait_ge(s_out, 16 * STORES)
            for i in range(2):
                act.dma_start(bias_raw[i * E:(i + 1) * E, 0:2 * FF], b_up[0]).then_inc(ld["bias"], 16)
                act.dma_start(bias_raw[i * E:(i + 1) * E, 2 * FF:], b_down[0]).then_inc(ld["bias"], 16)
            act.dma_start(w_proj_sb[:], w_ple_proj.rearrange("a (k p) n -> p (a k) n", p=P)).then_inc(ld["ple"], 16)
            act.dma_start(p_sb[:, 0:LAST, :], p_prompt[0, 0].rearrange("(t p) n -> p t n", p=P)).then_inc(ld["p"], 16)
            act.wait_ge(s_p0, 1)
            act.dma_start(p_sb[0:NS, LAST, :], p_sample.rearrange("a b s n -> (a b s) n")).then_inc(ld["p"], 16)

            def square2(t):
                act.wait_ge(s_emptied["V"], EMPTIED[("out", t)])
                act.wait_ge(s_sq, TT + t)
                act.activation(junk[:], resid[:, t, :], ACT.Square, accum_out=sq2[:, t:t + 1]).then_inc(s_sq, 1)

            square2(0)
            for t in range(TT):
                if t + 1 < TT:
                    square2(t + 1)
                if t >= 2:
                    act.wait_ge(s_job, JOB[("logits", t - 2)] + 1)
                job_filled(act, ("h2T", t))
                act.activation(h2T[:, t % 2, :, :], banks(("h2T", t)).rearrange("p a (b n) -> p (a b) n", n=P),
                               ACT.Copy).then_inc(s_emptied["A"], 1)
            act.wait_ge(ld["bias"], 64)
            act.activation(bias_hl[0:2 * E, :], bias_raw[0:2 * E, :], ACT.Copy).then_inc(s_bias, 1)
            for t in range(TT):
                act.wait_ge(s_top, t + 1)
                act.activation(exps[:, t, :], top8[:, t, 0:TOPK], ACT.Exp, bias=neg_max[:, t:t + 1],
                               accum_out=exp_sum[:, t:t + 1]).then_inc(s_exp, 1)
            for t in range(TT):
                job_filled(act, ("pT", t))
                act.activation(pT[:, :, t * P:(t + 1) * P], bank(("pT", t))[:, 0:PD].rearrange("p (k n) -> p k n", n=P),
                               ACT.Copy).then_inc(s_emptied["A"], 1)
            for t in range(TT):
                job_filled(act, ("ple", t))
                act.activation(ple[:, t, :], banks(("ple", t)).rearrange("p a n -> p (a n)"),
                               ACT.Copy).then_inc(s_emptied["A"], 1)

            act.wait_ge(s_route, 1)

            def hi_part(J, s):
                wait_landed(act, J, s)
                if not (isinstance(J, int) and STEP_CHUNKS * J + s < SPLIT):
                    act.wait_ge(s_chunk, STEP_CHUNKS * J + s - SPLIT + 1)
                act.activation(w_hi[:, s % SPLIT, :], raw[:, s % RING, :], ACT.Copy).then_inc(s_hi, 1)

            def xT_high(u):
                act.wait_ge(s_xtp, u + 1)
                act.activation(xT_hi[:].rearrange("p k n -> p (k n)"), tp, ACT.Copy).then_inc(s_xhi, 1)

            def aT_high(u):
                act.wait_ge(s_atp, u + 1)
                act.activation(aT_hi[:].rearrange("p k n -> p (k n)"), tp, ACT.Copy).then_inc(s_ahi, 1)

            def sigmoid(u):
                act.wait_ge(s_glu, u + 1)
                act.activation(sig[:], glu[:], ACT.Sigmoid, scale=ALPHA).then_inc(s_sig, 1)

            def y_out(u, chunks):
                act.wait_ge(s_chunk, chunks)
                if not (isinstance(u, int) and u == 0):
                    act.wait_ge(s_scat, 16 * u)
                act.activation(y_rows[:], dn, ACT.Copy).then_inc(s_y, 1)

            def step(J, has_y=True):
                for x in range(STEP_CHUNKS):
                    hi_part(J, UP_CHUNKS + x)
                    if x == 2 and has_y:
                        y_out(J - 1, STEP_CHUNKS * J + UP_CHUNKS)
                    if x == 4:
                        aT_high(J)
                    if x == 10:
                        sigmoid(J + 1)
                xT_high(J + 2)

            act.wait_ge(s_moe, 1)
            for s in range(2):
                hi_part(0, s)
            xT_high(0)
            for s in range(2, UP_CHUNKS):
                hi_part(0, s)
            sigmoid(0)
            xT_high(1)
            step(0, has_y=False)
            step(1)
            with act.Fori(2, E - 1) as J:
                step(J)
            n_over = act.value_load(over_i[0:1, 0:1], min_val=0, max_val=OVER)
            with act.Fori(0, OVER) as b:
                with act.If(b < n_over):
                    step(b + (E - 1))
            hi_part(n_over + (E - 1), UP_CHUNKS)
            hi_part(n_over + (E - 1), UP_CHUNKS + 1)
            hi_part(n_over + (E - 1), UP_CHUNKS + 2)
            y_out(n_over + (E - 2), (n_over + (E - 1)) * STEP_CHUNKS + UP_CHUNKS)
            aT_high(n_over + (E - 1))
            hi_part(n_over + (E - 1), UP_CHUNKS + 3)
            y_out(n_over + (E - 1), (n_over + (E - 1)) * STEP_CHUNKS + STEP_CHUNKS)

            for t in range(TT):
                act.wait_ge(s_x2tp, t + 1)
                if t >= 2:
                    act.wait_ge(s_gmm, t - 1)
                act.activation(x2T[:, t % 2, :, :].rearrange("p k n -> p (k n)"), ps[:, 4 + 2 * (t % 2):6 + 2 * (t % 2), :].rearrange("p a n -> p (a n)"),
                               ACT.Copy).then_inc(s_x2T, 1)
                if t >= 1:
                    tail_gate(act, t - 1)
            tail_gate(act, LAST)

        @block.tensor
        def _(pe):
            pe.wait_ge(s_ident, 1)

            def transposes(name, src):
                job_free(pe, name)
                for k in range(KD):
                    mm = pe.transpose(bank(name, k // 4)[:, (k % 4) * P:(k % 4 + 1) * P], src[:, k * P:(k + 1) * P], ident[:])
                mm.then_inc(s_job, 1)

            for t in range(TT):
                pe.wait_ge(s_xn, t + 1)
                transposes(("xT", t), xn[:, t % 2, :])
            name = ("misc", 0)
            job_free(pe, name)
            pe.wait_ge(s_wpart, 1)
            pe.wait_ge(ld["state"], 32)
            for h in range(G):
                pe.transpose(bank(name)[:, h * P:(h + 1) * P], sgu_w_sb[:, h, :], ident[:])
            n = DB * PB
            for g in range(G):
                pe.transpose(bank(name, 1)[:, g * n:(g + 1) * n], state_sb[0:n, g * P:(g + 1) * P], ident[0:n, 0:n])
            pe.transpose(bank(name, 1)[:, G * n:G * n + G], scale4[:], ident[0:G, 0:G]).then_inc(s_job, 1)
            name = ("blockw", 0)
            job_free(pe, name)
            pe.wait_ge(s_chain, 1)
            pe.wait_ge(s_emptied["V"], EMPTIED[("misc", 0)])
            for h in range(G):
                mm = pe.matmul(bank(name)[0:NS, h * DS:(h + 1) * DS], rep[0:DS, :], wsT[0:DS, h, 0:DS], start=True, stop=True)
            mm.then_inc(s_job, 1)
            pe.wait_ge(ld["w_in_v"], 16 * (KD // 2))
            pe.wait_ge(s_emptied["A"], EMPTIED[("xT", LAST)])
            for t in range(TT):
                name = ("v", t)
                job_free(pe, name)
                for k in range(KD):
                    mm = pe.matmul(bank(name), actsT[:, k, t * P:(t + 1) * P], w_in_sb[:, k, PW + SG:],
                                   start=(k == 0), stop=(k == KD - 1))
                mm.then_inc(s_job, 1)
            pe.wait_ge(ld["w_in_z"], 16 * (KD // 2))
            for m in range(2 * G):
                name = ("z", m)
                job_free(pe, name)
                for k in range(KD):
                    w = w_in_sb[:, k, m * P:(m + 1) * P]
                    pe.matmul(bank(name), w, actsT[:, k, 0:SEQ], start=(k == 0), stop=(k == KD - 1))
                    mm = pe.matmul(bank(name, 1)[:, 0:NS], w, actsT[:, k, SEQ:T], start=(k == 0), stop=(k == KD - 1))
                mm.then_inc(s_job, 1)
            name = ("newpool", 0)
            job_free(pe, name)
            pe.wait_ge(s_emptied["A"], EMPTIED[("z", G - 1)])
            for g in range(G):
                pe.transpose(bank(name)[0:PB, g * P:(g + 1) * P], ext[:, g, LEAD + SEQ - PB:LEAD + SEQ], ident[:])
            for g in range(G):
                mm = pe.transpose(bank(name, 1)[0:NS, g * P:(g + 1) * P], new_cols[:, g, :], ident[:])
            mm.then_inc(s_job, 1)
            pe.wait_ge(ld["pool_w"], 16)
            for g in range(G):
                name = ("pool", g)
                job_free(pe, name)
                pe.wait_ge(s_diff, g + 1)
                pe.matmul(bank(name), w_pool_sb[:, g, :], diff[:, 0:SEQ], start=True, stop=True)
                pe.matmul(bank(name, 1)[:, 0:NS], w_pool_sb[:, g, :], diff[:, SEQ:T], start=True, stop=True).then_inc(s_job, 1)
            pe.wait_ge(s_emptied["V"], EMPTIED[("blockw", 0)])
            for t in range(TT):
                name = ("gating", t)
                job_free(pe, name)
                pe.wait_ge(s_v, t + 1)
                for h in range(G):
                    v = v_sb[0:NT[t], t, h * P:(h + 1) * P]
                    w = wsT[:, h, :] if t < LAST else block_w[0:NS, h, :]
                    mm = pe.matmul(bank(name)[:, h * NT[t]:(h + 1) * NT[t]], v, w, start=True, stop=True)
                mm.then_inc(s_job, 1)
            pe.wait_ge(ld["w_out"], 16)
            pe.wait_ge(s_mix, G + TT)
            pe.wait_ge(s_pad, 1)
            pe.wait_ge(ld["router"], 32)
            pe.wait_ge(s_const, 14)
            for i in range(TT + 2):
                if i < TT:
                    name = ("out", i)
                    job_free(pe, name)
                    for b in range(2):
                        for k in range(KD):
                            mm = pe.matmul(bank(name, b), actsT[:, k, i * P:(i + 1) * P], w_out_sb[:, k, b * 512:(b + 1) * 512],
                                           start=(k == 0), stop=(k == KD - 1))
                    mm.then_inc(s_job, 1)
                if 0 <= i - 1 < TT:
                    pe.wait_ge(s_xn, TT + i)
                    transposes(("h2T", i - 1), xn[:, (i - 1) % 2, :])
                if 0 <= i - 2 < TT:
                    t = i - 2
                    name = ("logits", t)
                    job_free(pe, name)
                    pe.wait_ge(s_emptied["A"], EMPTIED[("h2T", t)])
                    pe.matmul(bank(name)[:, 0:E], ones[0:1, :], b_router_sb[:], start=True, stop=False)
                    for k in range(KD):
                        mm = pe.matmul(bank(name)[:, 0:E], h2T[:, t % 2, k, :], w_router_sb[:, k, :], start=False, stop=(k == KD - 1))
                    mm.then_inc(s_job, 1)
            name = ("rank", 0)
            job_free(pe, name)
            pe.wait_ge(s_mask, TT)
            rk = bank(name)[:, 0:TT * E]
            pe.matmul(rk, before[:], mask[:].rearrange("p t e -> p (t e)"), start=True, stop=False)
            for t in range(LAST):
                n = LAST - t
                pe.matmul(rk[:, (t + 1) * E:].rearrange("p (t e) -> p t e", e=E), ones[:],
                          mask[:, t:t + 1, :].to_broadcast([P, n, E]), start=False, stop=(t == LAST - 1))
            for t in range(TT):
                mm = pe.matmul(bank(name, 1)[:, 0:E], ones[:], mask[:, t, :], start=(t == 0), stop=(t == LAST))
            mm.then_inc(s_job, 1)
            pe.wait_ge(ld["ple"], 16)
            pe.wait_ge(ld["p"], 32)
            for t in range(TT):
                name = ("pT", t)
                job_free(pe, name)
                for k in range(KP):
                    mm = pe.transpose(bank(name)[:, k * P:(k + 1) * P], p_sb[:, t, k * P:(k + 1) * P], ident[:])
                mm.then_inc(s_job, 1)
            for t in range(TT):
                name = ("ple", t)
                job_free(pe, name)
                pe.wait_ge(s_emptied["A"], EMPTIED[("pT", t)])
                for b in range(2):
                    for k in range(KP):
                        mm = pe.matmul(bank(name, b), pT[:, k, t * P:(t + 1) * P], w_proj_sb[:, k, b * 512:(b + 1) * 512],
                                       start=(k == 0), stop=(k == KP - 1))
                mm.then_inc(s_job, 1)

            pe.wait_ge(s_emptied["A"], TOTAL["A"])
            pe.wait_ge(s_emptied["V"], TOTAL["V"])

            def slots(u):
                pe.wait_ge(s_picks, u + 1)
                if not (isinstance(u, int) and u == 0):
                    pe.wait_ge(s_rows, u)
                if not (isinstance(u, int) and u <= 2):
                    pe.wait_ge(s_y, u - 2)
                for t in range(TT):
                    mm = pe.matmul(slot_sum, picks[:, t, :], tok_slot[:, 1, t:t + 1], start=(t == 0), stop=(t == LAST))
                mm.then_inc(s_rowps, 1)

            def x_transposes(u):
                pe.wait_ge(s_gather, 16 * u + 16)
                if not (isinstance(u, int) and u <= 1):
                    pe.wait_ge(s_alo, u - 1)
                elif u == 1:
                    pe.wait_ge(s_xlo, 1)
                for k in range(KD):
                    mm = pe.transpose(tp[:, k * P:(k + 1) * P], x_rows[:, k * P:(k + 1) * P], ident[:])
                mm.then_inc(s_xtp, 1)

            def a_transposes(u):
                pe.wait_ge(s_act, u + 1)
                pe.wait_ge(s_xlo, u + 2)
                for k in range(KD):
                    mm = pe.transpose(tp[:, k * P:(k + 1) * P], lin[:, k * P:(k + 1) * P], ident[:])
                mm.then_inc(s_atp, 1)

            def bias(out, oh, lo, hi):
                for c in range(lo, hi, 512):
                    pe.matmul(out[:, c - lo:c - lo + 512], oh[:], bias_hl[:, c:c + 512], start=True, stop=False,
                              skip_group_check=True)

            def products(J, s, out, parts, last):
                wait_hi(pe, J, s)
                for xs in (0, 1):
                    for k, (xh, xl, base, width) in enumerate(parts):
                        for c in range(0, width, 512):
                            pe.matmul(out[:, c:c + 512], (xh, xl)[xs], w_hi[:, s % SPLIT, base + c:base + c + 512],
                                      start=False, stop=False, skip_group_check=True)
                wait_lo(pe, J, s)
                for k, (xh, xl, base, width) in enumerate(parts):
                    for c in range(0, width, 512):
                        mm = pe.matmul(out[:, c:c + 512], xh, w_lo[:, s % SPLIT, base + c:base + c + 512],
                                       start=False, stop=last and k == len(parts) - 1, skip_group_check=True)
                mm.then_inc(s_chunk, 1)

            def up_start(u):
                pe.wait_ge(s_xhi, u + 1)
                pe.wait_ge(s_xlo, u + 1)
                pe.wait_ge(s_oh, u + 1)
                if not (isinstance(u, int) and u == 0):
                    pe.wait_ge(s_lin, u)
                    pe.wait_ge(s_glu, u)
                bias(gu, oh_up, 0, 2 * FF)

            def up_chunk(J, s, c):
                products(J, s, gu, [(xT_hi[:, c, :], xT_lo[:, c, :], 0, 2 * FF)], c == UP_CHUNKS - 1)

            def dn_start(u, found):
                pe.wait_ge(s_ahi, u + 1)
                pe.wait_ge(s_alo, u + 1)
                pe.wait_ge(s_oh, u + 2)
                pe.wait_ge(s_rows, found)
                if not (isinstance(u, int) and u == 0):
                    pe.wait_ge(s_y, u)
                bias(dn, oh_dn, 2 * FF, 2 * FF + D)

            def dn_chunk(J, s, c):
                products(J, s, dn, [(aT_hi[:, 2 * c + j, :], aT_lo[:, 2 * c + j, :], j * D, D) for j in range(2)],
                         c == DN_CHUNKS - 1)

            def step(J):
                up_start(J + 1)
                for c in range(UP_CHUNKS):
                    up_chunk(J, UP_CHUNKS + c, c)
                    if c == 1:
                        a_transposes(J)
                    if c == 3:
                        slots(J + 2)
                for c in range(DN_CHUNKS):
                    if c == 0:
                        dn_start(J, J + 3)
                    dn_chunk(J, 2 * UP_CHUNKS + c, c)
                    if c == 0:
                        x_transposes(J + 2)

            pe.wait_ge(s_bias, 2)
            slots(0)
            x_transposes(0)
            up_start(0)
            for c in range(UP_CHUNKS):
                up_chunk(0, c, c)
                if c == 3:
                    slots(1)
            x_transposes(1)
            step(0)
            step(1)
            with pe.Fori(2, E - 1) as J:
                step(J)
            n_over = pe.value_load(over_i[0:1, 0:1], min_val=0, max_val=OVER)
            with pe.Fori(0, OVER) as b:
                with pe.If(b < n_over):
                    step(b + (E - 1))
            J = n_over + (E - 1)
            a_transposes(J)
            dn_start(J, J + 2)
            for c in range(DN_CHUNKS):
                dn_chunk(J, UP_CHUNKS + c, c)

            pe.wait_ge(s_y, n_over + E)
            for t in range(TT):
                pe.wait_ge(s_comb, t + 1)
                if t >= 2:
                    pe.wait_ge(s_x2T, t - 1)
                for k in range(KD):
                    mm = pe.transpose(ps[:, 4 + 2 * (t % 2) + k // 4, (k % 4) * P:(k % 4 + 1) * P],
                                      resid[:, t, k * P:(k + 1) * P], ident[:])
                mm.then_inc(s_x2tp, 1)
                if t >= 1:
                    gate_product(pe, t - 1)
            gate_product(pe, LAST)

        @block.vector
        def _(dve):
            chain = [0]

            def link(ins):
                chain[0] += 1
                ins.then_inc(s_chain, 1)
                dve.wait_ge(s_chain, chain[0])

            dve.wait_ge(s_ident, 1)
            link(dve.tensor_copy(rep[0:DS, :].rearrange("p (b s) -> p b s", b=DB),
                                 ident[0:DS, 0:DS].rearrange("p (o s) -> p o s", o=1).to_broadcast([DS, DB, DS])))
            for t in range(TT):
                dve.wait_ge(s_sq, t + 1)
                dve.tensor_scalar(var1[:, t:t + 1], sq1[:, t:t + 1], 1.0 / D, NORM_EPS, ALU.mult, ALU.add).then_inc(s_var, 1)
            dve.wait_ge(ld["gain"], 16)
            for t in range(TT):
                dve.wait_ge(s_rstd, t + 1)
                if t >= 2:
                    job_filled(dve, ("xT", t - 2))
                dve.scalar_tensor_tensor(out=xn[:, t % 2, :], in0=resid[:, t, :], scalar=rstd1[:, t:t + 1], in1=gain[:],
                                         op0=ALU.mult, op1=ALU.mult).then_inc(s_xn, 1)
            name = ("misc", 0)
            job_filled(dve, name)
            dve.wait_ge(s_ext0, 2)
            dve.tensor_copy(wsT[:].rearrange("p h i -> p (h i)"), bank(name))
            n = DB * PB
            for g in range(G):
                dve.tensor_copy(ext[:, g, LEAD + SEQ:].rearrange("p (b s) -> p b s", b=DB)[:, :, 1:LEAD],
                                bank(name, 1)[:, g * n:(g + 1) * n].rearrange("p (b r) -> p b r", b=DB))
            dve.tensor_copy(scaleT[:], bank(name, 1)[:, G * n:G * n + G]).then_inc(s_emptied["V"], 1)
            name = ("blockw", 0)
            job_filled(dve, name)
            dve.wait_ge(s_wpart, 2)
            for h in range(G):
                few = bank(name)[0:NS, h * DS:(h + 1) * DS].rearrange("p (o s) -> p o s", o=1).to_broadcast([NS, DB, DS])
                ins = dve.tensor_tensor(block_w[0:NS, h, :].rearrange("p (b s) -> p b s", b=DB), few, same_seq[0:NS], ALU.mult)
            ins.then_inc(s_emptied["V"], 1)
            dve.wait_ge(s_const, 1 + G)
            link(dve.reciprocal(head_fix[:], head_fix[:]))
            for g, w in enumerate(WINDOWS):
                ins = dve.tensor_scalar(head_fix[:, g, :], head_fix[:, g, :], float(w), None, ALU.mult)
            link(ins)

            def layernorm_stats(t):
                n = NT[t]
                dve.wait_ge(s_emptied["A"], EMPTIED[("v", t)])
                for h in range(G):
                    ins = dve.bn_stats(stats[0:n, h, :], v_sb[0:n, t, h * P:(h + 1) * P])
                link(ins)
                for h in range(G):
                    ins = dve.bn_aggr(mean_var[0:n, t, h, :], stats[0:n, h, :])
                link(ins)
                dve.tensor_scalar(ln_var[0:n, t, :], mean_var[0:n, t, :, 1], LN_EPS, None, ALU.add).then_inc(s_lnv, 1)

            def difference(g):
                w = 1.0 / WINDOWS[g]
                dve.wait_ge(s_sum, g + 1)
                if g >= 1:
                    job_filled(dve, ("pool", g - 1))
                link(dve.tensor_tensor(sumA[:, LEAD:2 * LEAD], sumA[:, LEAD:2 * LEAD], head_fix[:, g, :], ALU.mult))
                dve.scalar_tensor_tensor(out=diff[:, 0:SEQ], in0=sumA[:, LEAD:LEAD + SEQ], scalar=w,
                                         in1=ext[:, g, LEAD:LEAD + SEQ], op0=ALU.mult, op1=ALU.subtract)

                def new(a):
                    return a.rearrange("p (b s) -> p b s", b=DB)[:, :, LEAD:]
                dve.scalar_tensor_tensor(out=diff[:, SEQ:T].rearrange("p (b s) -> p b s", b=DB),
                                         in0=new(sumA[:, LEAD + SEQ:]), scalar=w, in1=new(ext[:, g, LEAD + SEQ:]),
                                         op0=ALU.mult, op1=ALU.subtract).then_inc(s_diff, 1)

            def pool_out(g):
                name = ("pool", g)
                job_filled(dve, name)
                dve.tensor_scalar(actsT[:, g, 0:SEQ], bank(name), scaleT[:, g:g + 1], None, ALU.mult).then_inc(s_mix, 1)
                dve.tensor_scalar(actsT[:, g, SEQ:T], bank(name, 1)[:, 0:NS], scaleT[:, g:g + 1], None,
                                  ALU.mult).then_inc(s_emptied["V"], 1)

            dve.wait_ge(ld["ln"], 32)
            dve.wait_ge(ld["small"], 16)
            for t in range(TT):
                layernorm_stats(t)
            for g in range(G):
                difference(g)
                pool_out(g)
            dve.memset(actsT[:, :, T:], 0.0).then_inc(s_pad, 1)
            for t in range(TT):
                n = NT[t]
                dve.wait_ge(s_lnr, t + 1)
                for h in range(G):
                    v = v_sb[0:n, t, h * P:(h + 1) * P]
                    ins = dve.tensor_scalar(v, v, mean_var[0:n, t, h, 0:1], ln_rstd[0:n, t, h:h + 1], ALU.subtract, ALU.mult)
                link(ins)
                v = v_sb[0:n, t, :]
                link(dve.tensor_tensor(v, v, ln_g[0:n, :], ALU.mult))
                dve.tensor_tensor(v, v, ln_b[0:n, :], ALU.add).then_inc(s_v, 1)
            for t in range(TT):
                name = ("gating", t)
                n = NT[t]
                job_filled(dve, name)
                dve.wait_ge(s_mix, G + t)
                got = gated[:, 0:G * n].rearrange("p (h n) -> p h n", h=G)
                src = bank(name)[:, 0:G * n]
                if t < LAST:
                    add = dve.tensor_tensor(got, src.rearrange("p (h n) -> p h n", h=G), sgu_bias[:], ALU.add)
                    add.then_inc(s_emptied["V"], 1)
                else:
                    for h in range(G):
                        add = dve.tensor_tensor(
                            gated[:, h * n:(h + 1) * n].rearrange("p (b s) -> p b s", b=DB),
                            src[:, h * n:(h + 1) * n].rearrange("p (b s) -> p b s", b=DB),
                            sgu_bias[:, h:h + 1, 0:DS].to_broadcast([P, DB, DS]), ALU.add)
                    add.then_inc(s_emptied["V"], 1)
                dve.wait_ge(s_emptied["V"], EMPTIED[name])
                dve.tensor_tensor(actsT[:, G:2 * G, t * P:t * P + n], got, uT[:, :, t * P:t * P + n],
                                  ALU.mult).then_inc(s_mix, 1)
            dve.wait_ge(s_mix, G + TT)
            dve.memset(p_sb[:, LAST, :], 0.0).then_inc(s_p0, 1)

            def logits_top(t):
                name = ("logits", t)
                job_filled(dve, name)
                dve.tensor_copy(logits[:, t, :], bank(name)[:, 0:E]).then_inc(s_emptied["V"], 1)
                dve.wait_ge(s_emptied["V"], EMPTIED[name])
                link(dve.max(top8[:, t, :], logits[:, t, :]))
                link(dve.max_index(top_i[:, t, :], top8[:, t, :], logits[:, t, :]))
                dve.tensor_scalar(neg_max[:, t:t + 1], top8[:, t, 0:1], -1.0, None, ALU.mult).then_inc(s_top, 1)
                link(dve.tensor_copy(top_f[:, t, :], top_i[:, t, 0:TOPK]))
                link(dve.tensor_tensor(chosen[:, t, :, :],
                                       expert_iota[:].rearrange("p (o e) -> p o e", o=1).to_broadcast([P, TOPK, E]),
                                       top_f[:, t, :].rearrange("p (k o) -> p k o", o=1).to_broadcast([P, TOPK, E]),
                                       ALU.is_equal))
                dve.tensor_reduce(mask[0:NT[t], t, :], chosen[0:NT[t], t, :, :].rearrange("p k e -> p e k"), AX.X,
                                  ALU.add).then_inc(s_mask, 1)

            dve.wait_ge(ld["gain2"], 16)
            dve.wait_ge(s_const, 14)
            for i in range(TT + 2):
                if i < TT:
                    name = ("out", i)
                    job_filled(dve, name)
                    for b in range(2):
                        x = resid[:, i, b * 512:(b + 1) * 512]
                        ins = dve.tensor_tensor(x, x, bank(name, b), ALU.add)
                    ins.then_inc(s_emptied["V"], 1)
                if 0 <= i - 2 < TT:
                    logits_top(i - 2)
                if i < TT:
                    dve.wait_ge(s_sq, TT + i + 1)
                    dve.tensor_scalar(var2[:, i:i + 1], sq2[:, i:i + 1], 1.0 / D, NORM_EPS, ALU.mult, ALU.add).then_inc(s_var, 1)
                    dve.wait_ge(s_rstd, TT + i + 1)
                    if i >= 2:
                        job_filled(dve, ("h2T", i - 2))
                        dve.wait_ge(s_xrow[i - 2], 16)
                    dve.scalar_tensor_tensor(out=xn[:, i % 2, :], in0=resid[:, i, :], scalar=rstd2[:, i:i + 1], in1=gain2[:],
                                             op0=ALU.mult, op1=ALU.mult).then_inc(s_xn, 1)

            name = ("rank", 0)
            job_filled(dve, name)
            dve.tensor_copy(count[:], bank(name, 1)[:, 0:E])
            dve.tensor_copy(rank[:].rearrange("p t e -> p (t e)"), bank(name)[:, 0:TT * E]).then_inc(s_emptied["V"], 1)
            dve.wait_ge(s_emptied["V"], EMPTIED[name])
            link(dve.tensor_scalar(over[:], count[:], float(P + 1), None, ALU.is_ge))
            link(dve.tensor_scalar(depth[:], rank[:], float(P), None, ALU.is_ge))
            link(dve.tensor_copy(first[:], depth[:]))
            for m in range(2, TT):
                dve.scalar_tensor_tensor(out=over[:], in0=count[:], scalar=float(m * P + 1), in1=over[:],
                                         op0=ALU.is_ge, op1=ALU.add)
                link(dve.scalar_tensor_tensor(out=depth[:], in0=rank[:], scalar=float(m * P), in1=depth[:],
                                              op0=ALU.is_ge, op1=ALU.add))
            link(dve.tensor_tensor_scan(over_end[:], ones[:, 0:E], over[:], 0.0, ALU.mult, ALU.add))
            dve.tensor_copy(over_i[:], over_end[:, E - 1:E])
            link(dve.tensor_tensor(over_from[:], over_end[:], over[:], ALU.subtract))
            link(dve.tensor_tensor(over_from[:], over_from[:], expert_iota[:], ALU.subtract))
            link(dve.tensor_scalar(over_from[:], over_from[:], float(E - 1), None, ALU.add))

            def by_tile(a):
                return a.rearrange("p (o e) -> p o e", o=1).to_broadcast([P, TT, E])
            link(dve.tensor_tensor(first[:], first[:], by_tile(over_from[:]), ALU.mult))
            link(dve.tensor_tensor(first[:], first[:], depth[:], ALU.add))
            link(dve.tensor_tensor(first[:], first[:], by_tile(expert_iota[:]), ALU.add))
            link(dve.scalar_tensor_tensor(out=first[:], in0=first[:], scalar=1.0, in1=mask[:], op0=ALU.add, op1=ALU.mult))
            link(dve.tensor_scalar(block_of[:], first[:], -1.0, None, ALU.add))
            link(dve.scalar_tensor_tensor(out=pos_row[:, 0], in0=depth[:], scalar=float(-P), in1=rank[:], op0=ALU.mult, op1=ALU.add))
            link(dve.tensor_scalar(pos_row[:, 0], pos_row[:, 0], 1.0, None, ALU.add))
            link(dve.tensor_tensor(chosen_row[:], chosen[:],
                                   row_code[:].rearrange("p t (k o) -> p t k o", o=1).to_broadcast([P, TT, TOPK, E]), ALU.mult))
            for t in range(TT):
                ins = dve.tensor_reduce(pos_row[:, 1, t, :], chosen_row[:, t].rearrange("p k e -> p e k"), AX.X, ALU.add)
            link(ins)
            dve.tensor_copy(block_expert[:, 0:E], expert_iota[:])
            link(dve.tensor_tensor(over_cmp[:], over_end[:].rearrange("p (o e) -> p o e", o=1).to_broadcast([P, OVER + 2, E]),
                                   block_iota[:, 0:OVER + 2].rearrange("p (b o) -> p b o", o=1).to_broadcast([P, OVER + 2, E]),
                                   ALU.is_le))
            link(dve.tensor_reduce(block_expert[:, E:], over_cmp[:], AX.X, ALU.add))
            link(dve.tensor_copy(block_expert_i[:], block_expert[:]))
            dve.wait_ge(s_bias, 1)
            dve.tensor_tensor(bias_hl[E:2 * E, :], bias_raw[E:2 * E, :], bias_hl[E:2 * E, :].bitcast(F32), ALU.subtract)
            dve.memset(bias_hl[2 * E:P, :].bitcast(F32), 0.0).then_inc(s_bias, 1)
            dve.wait_ge(s_exp, TT)
            link(dve.reciprocal(exp_rcp[:], exp_sum[:]))
            dve.tensor_tensor(topw[:], exps[:], exp_rcp[:].rearrange("p (t o) -> p t o", o=1).to_broadcast([P, TT, TOPK]), ALU.mult).then_inc(s_route, 1)

            dve.wait_ge(s_emptied["A"], TOTAL["A"])
            dve.wait_ge(s_moe, 1)
            LINKS = 5 + 2 + 1
            moe = {"base": 0, "n": 0}

            def mlink(ins):
                moe["n"] += 1
                ins.then_inc(s_chain, 1)
                dve.wait_ge(s_chain, moe["base"] + moe["n"])

            def find(u):
                mlink(dve.tensor_scalar(same_block[:], block_of[:], cur_block[:, 0:1], None, ALU.is_equal))
                mlink(dve.tensor_tensor(in_block[:], pos_row[:],
                                        same_block[:].rearrange("p (o t) e -> p o t e", o=1).to_broadcast([P, 2, TT, E]), ALU.mult))
                mlink(dve.tensor_reduce(tok_slot[:], in_block[:], AX.X, ALU.add))
                for t in range(TT):
                    ins = dve.tensor_scalar(picks[:, t, :], slot1[:], tok_slot[:, 0, t:t + 1], None, ALU.is_equal)
                ins.then_inc(s_picks, 1)
                mlink(dve.scalar_tensor_tensor(out=junk_b[:], in0=block_iota[:], scalar=cur_block[:, 0:1], in1=block_expert[:],
                                               op0=ALU.is_equal, op1=ALU.mult, accum_out=cur_expert[:]))
                mlink(dve.tensor_scalar(cur_block[:], cur_block[:], 1.0, None, ALU.add))

            def row_numbers(u):
                dve.wait_ge(s_rowps, u + 1)
                if not (isinstance(u, int) and u == 0):
                    dve.wait_ge(s_gather, 16 * u)
                mlink(dve.tensor_copy(rows_tmp[:], rows[:, 0:3]))
                dve.tensor_copy(rows[:, 1:4], rows_tmp[:])
                mlink(dve.tensor_scalar(rows[:, 0:1], slot_sum, float(NO_ROW), None, ALU.add))
                dve.tensor_scalar(token_of[:], rows[:, 0:1], 2, None, ALU.logical_shift_right).then_inc(s_rows, 1)

            def bias_picks(u):
                mlink(dve.tensor_copy(oh_dn[:], oh_up[:].bitcast(F32)))
                dve.tensor_scalar(oh_up[:], bias_row[:, 0:1].to_broadcast([P, P]), cur_expert[:, 0:1], None,
                                  ALU.is_equal).then_inc(s_oh, 1)

            def lo_part(J, s):
                wait_hi(dve, J, s)
                dve.tensor_tensor(w_lo[:, s % SPLIT, :], raw[:, s % RING, :], w_hi[:, s % SPLIT, :].bitcast(F32),
                                  ALU.subtract).then_inc(s_lo["V"], 1)

            def xT_low(u):
                dve.wait_ge(s_xhi, u + 1)
                dve.tensor_tensor(xT_lo[:].rearrange("p k n -> p (k n)"), tp, xT_hi[:].rearrange("p k n -> p (k n)").bitcast(F32),
                                  ALU.subtract).then_inc(s_xlo, 1)

            def aT_low(u):
                dve.wait_ge(s_ahi, u + 1)
                dve.tensor_tensor(aT_lo[:].rearrange("p k n -> p (k n)"), tp, aT_hi[:].rearrange("p k n -> p (k n)").bitcast(F32),
                                  ALU.subtract).then_inc(s_alo, 1)

            def clamps(u, chunks):
                dve.wait_ge(s_chunk, chunks)
                dve.tensor_scalar(glu[:], gu[:, 0:FF], LIMIT, None, ALU.min).then_inc(s_glu, 1)
                dve.tensor_scalar(lin[:], gu[:, FF:], LIMIT, -LIMIT, ALU.min, ALU.max).then_inc(s_lin, 1)

            def activation(u):
                dve.wait_ge(s_gs, u + 1)
                dve.wait_ge(s_lin, u + 1)
                dve.scalar_tensor_tensor(out=lin[:], in0=lin[:], scalar=1.0, in1=sig[:], op0=ALU.add,
                                         op1=ALU.mult).then_inc(s_act, 1)

            def step(J):
                moe["n"] = 0
                for x in range(STEP_CHUNKS):
                    s = UP_CHUNKS + x
                    if x == 1:
                        find(J + 2)
                    if lo_by(s) == "V":
                        lo_part(J, s)
                    if x == 4:
                        aT_low(J)
                    if x == 6:
                        row_numbers(J + 2)
                    if x == 10:
                        clamps(J + 1, STEP_CHUNKS * J + 2 * UP_CHUNKS)
                activation(J + 1)
                bias_picks(J + 2)
                xT_low(J + 2)
                assert moe["n"] == LINKS

            mlink_start = chain[0]
            moe["base"] = mlink_start
            mlink(dve.memset(rows[:], NO_ROW))
            mlink(dve.memset(oh_up[:].bitcast(F32), 0.0))
            find(0)
            bias_picks(0)
            row_numbers(0)
            for s in range(2):
                if lo_by(s) == "V":
                    lo_part(0, s)
            xT_low(0)
            for s in range(2, UP_CHUNKS):
                if lo_by(s) == "V":
                    lo_part(0, s)
                if s == 2:
                    find(1)
                if s == 6:
                    row_numbers(1)
            clamps(0, UP_CHUNKS)
            activation(0)
            bias_picks(1)
            xT_low(1)
            before_steps = moe["base"] + moe["n"]
            moe["base"] = before_steps
            step(0)
            moe["base"] = before_steps + LINKS
            step(1)
            with dve.Fori(2, E - 1) as J:
                moe["base"] = J * LINKS + before_steps
                step(J)
            n_over = dve.value_load(over_i[0:1, 0:1], min_val=0, max_val=OVER)
            with dve.Fori(0, OVER) as b:
                with dve.If(b < n_over):
                    moe["base"] = (b + (E - 1)) * LINKS + before_steps
                    step(b + (E - 1))
            J = n_over + (E - 1)
            for x in range(3):
                if lo_by(UP_CHUNKS + x) == "V":
                    lo_part(J, UP_CHUNKS + x)
            aT_low(J)
            if lo_by(UP_CHUNKS + 3) == "V":
                lo_part(J, UP_CHUNKS + 3)

            dve.wait_ge(ld["gain_f"], 16)
            tail = [0]

            def tlink(ins):
                tail[0] += 1
                ins.then_inc(s_tchain, 1)
                dve.wait_ge(s_tchain, tail[0])

            def combine(t):
                n = NT[t]
                dve.wait_ge(s_yk[t % YB], 16 * (t // YB + 1))
                x = resid[0:n, t, :]
                yk = raw[0:n, 2 * (t % YB):2 * (t % YB) + 2, :].rearrange("p a (b d) -> p (a b) d", d=D)
                for k in range(TOPK):
                    ins = dve.scalar_tensor_tensor(out=x, in0=yk[:, k, :], scalar=topw[0:n, t, k:k + 1], in1=x,
                                                   op0=ALU.mult, op1=ALU.add)
                    if k < TOPK - 1:
                        tlink(ins)
                ins.then_inc(s_comb, 1)

            def finish(t):
                dve.wait_ge(s_gate, t + 1)
                dve.wait_ge(s_x2tp, t + 1)
                g = gate[:, t % 2, :]
                tlink(dve.tensor_tensor(g, g, ple[:, t, :], ALU.mult))
                dve.tensor_tensor(resid[:, t, :], resid[:, t, :], g, ALU.add).then_inc(s_x3, 1)
                dve.wait_ge(s_sq3, t + 1)
                dve.tensor_scalar(var3[:, t:t + 1], sq3[:, t:t + 1], 1.0 / D, NORM_EPS, ALU.mult, ALU.add).then_inc(s_var3, 1)
                dve.wait_ge(s_rstd3, t + 1)
                if t >= 2:
                    dve.wait_ge(s_ost[t % 2], 16 * (t // 2))
                dve.scalar_tensor_tensor(out=out_rows[:, t % 2, :], in0=resid[:, t, :], scalar=rstd3[:, t:t + 1], in1=gain_f[:],
                                         op0=ALU.mult, op1=ALU.mult).then_inc(s_orow, 1)

            for t in range(TT):
                combine(t)
                if t >= 2:
                    finish(t - 2)
            finish(LAST - 1)
            finish(LAST)


_INS = ["x_prompt", "x_sample", "state_pool", "p_prompt", "p_sample", "norm_mix", "w_in", "w_pool", "pool_scale",
        "sgu_ln_g", "sgu_ln_b", "sgu_w", "sgu_b", "w_out", "norm_ffn", "w_router", "b_router", "w_up", "b_up",
        "w_down", "b_down", "w_ple_gate", "w_ple_proj", "norm_final"]
_OUTS = [(1, 512, 1024), (8, 4, 1024), (1, 1, 15, 512), (1, 8, 15, 512), (1, 8, 4, 512)]


def kernel(**inputs):
    import numpy as _np
    import concourse.bacc as _bacc
    from concourse import mybir as _mybir
    from concourse.bass_utils import run_bass_kernel_spmd as _run

    nc = _bacc.Bacc("TRN2", target_bir_lowering=False, num_devices=1)
    arrays, args = {}, []
    for name in _INS:
        a = _np.ascontiguousarray(inputs[name])
        arrays[f"in_{name}_dram"] = a
        args.append(nc.dram_tensor(f"in_{name}_dram", a.shape, _mybir.dt.from_np(a.dtype), kind="ExternalInput").ap())
    for i, shape in enumerate(_OUTS):
        args.append(nc.dram_tensor(f"out_{i}_dram", shape, _mybir.dt.from_np(_np.dtype("float32")), kind="ExternalOutput").ap())
    build(nc, *args)
    r = _run(nc, [arrays], core_ids=[0])
    return tuple(r.results[0][f"out_{i}_dram"] for i in range(len(_OUTS)))
```

```python
from contextlib import ExitStack

import concourse.bass as bass
from concourse import mybir

F32 = mybir.dt.float32
F32R = mybir.dt.float32r
I32 = mybir.dt.int32
U32 = mybir.dt.uint32
ALU = mybir.AluOpType
ACT = mybir.ActivationFunctionType
AX = mybir.AxisListType

P = 128
RING = 6
SPLIT = 3
UP_CHUNKS = 8
DN_CHUNKS = 4
STEP_CHUNKS = UP_CHUNKS + DN_CHUNKS
POOL_LO = (4, 10)
FIRST_GATHER = 7
NO_ROW = 4096


def build(nc, x_prompt, x_sample, state_pool, p_prompt, p_sample, norm_mix, w_in, w_pool, pool_scale,
          sgu_ln_g, sgu_ln_b, sgu_w, sgu_b, w_out, norm_ffn, w_router, b_router, w_up, b_up, w_down,
          b_down, w_ple_gate, w_ple_proj, norm_final,
          y_prompt, y_sample, new_pool_prompt, new_pool_sample, new_sgu_v):
    SEQ, D = x_prompt.shape[1:]
    DB, DS = x_sample.shape[:2]
    NS = DB * DS
    T = SEQ + NS
    TT = SEQ // P + 1
    LAST = TT - 1
    NT = [P] * LAST + [NS]
    PW = state_pool.shape[3]
    PB = state_pool.shape[2]
    G = PW // P
    WINDOWS = (2, 4, 8, 16)
    KD = D // P
    IN = w_in.shape[2]
    SG = (IN - PW) // 2
    E = w_router.shape[2]
    FF = w_down.shape[2]
    TOPK = 4
    PD = w_ple_proj.shape[1]
    KP = PD // P
    OVER = T * TOPK // P - 1
    NBLK = E + OVER + 2
    LEAD = 16
    SB = LEAD + DS
    EXT = LEAD + SEQ + DB * SB
    NORM_EPS, LN_EPS = 1e-6, 1e-5
    LIMIT, ALPHA = 7.0, 1.702

    xn_dram = nc.dram_tensor("xn_rows", [T, D], F32, kind="Internal").ap()
    y4_dram = nc.dram_tensor("expert_rows", [T * TOPK, D], F32, kind="Internal").ap()
    up_dram = w_up.rearrange("a e (c p) n -> (a e c) p n", p=P)
    dn_dram = w_down.rearrange("a e (c j p) n -> (a e c) p j n", p=P, j=2)

    ctx = ExitStack()
    with ctx:
        def sb(name, shape, dt=F32, scope=ctx):
            return scope.enter_context(nc.sbuf_tensor(name, shape, dt))

        def sem(name):
            return ctx.enter_context(nc.semaphore(name))

        ident = sb("ident", [P, P])
        resid = sb("resid", [P, TT, D])
        topw = sb("topw", [P, TT, TOPK])
        block_of = sb("block_of", [P, TT, E])
        pos_row = sb("pos_row", [P, 2, TT, E])
        slot1 = sb("slot1", [P, P])
        block_iota = sb("block_iota", [P, NBLK])
        block_expert = sb("block_expert", [P, NBLK])
        block_expert_i = sb("block_expert_i", [P, NBLK], I32)
        over_i = sb("over_i", [P, 1], I32)
        cur_block = sb("cur_block", [P, 1])
        cur_expert = sb("cur_expert", [P, 1])
        bias_row = sb("bias_row", [P, 1])
        half_neg = sb("half_neg", [P, 16])
        with ExitStack() as s:
            xTh = sb("xTh", [P, KD, T], F32R, scope=s)
        with ExitStack() as s:
            bias_hl = sb("bias_hl", [P, 2 * FF + D], F32R, scope=s)
        gate_hi3 = sb("gate_hi3", [P, 2, D], F32R)
        junk_t = sb("junk_t", [P, D])
        x_rows = sb("x_rows", [P, D])
        picks = sb("picks", [P, TT, P])
        same_block = sb("same_block", [P, TT, E])
        in_block = sb("in_block", [P, 2, TT, E])
        tok_slot = sb("tok_slot", [P, 2, TT])
        junk_b = sb("junk_b", [P, NBLK])
        rows = sb("rows", [P, 4], U32)
        rows_tmp = sb("rows_tmp", [P, 3], U32)
        token_of = sb("token_of", [P, 1], U32)
        with ExitStack() as s:
            xT = sb("xT", [P, KD, TT * P], scope=s)
        with ExitStack() as s:
            xTl = sb("xTl", [P, KD, TT * P], F32R, scope=s)
        with ExitStack() as s:
            bias_raw = sb("bias_raw", [P, 2 * FF + D], scope=s)
        ple = sb("ple", [P, TT, D])
        with ExitStack() as s:
            w_v_sb = sb("w_v_sb", [P, KD, SG], scope=s)
            w_z_sb = sb("w_z_sb", [P, KD, PW], scope=s)
            w_u_sb = sb("w_u_sb", [P, KD, SG], scope=s)
        with ExitStack() as s:
            w_u_hi = sb("w_u_hi", [P, KD, SG], F32R, scope=s)
            w_z_lo = sb("w_z_lo", [P, KD, PW], F32R, scope=s)
            w_u_lo = sb("w_u_lo", [P, KD, SG], F32R, scope=s)
        with ExitStack() as s:
            w_out_b = sb("w_out_b", [P, KD // 2, D], scope=s)
            w_out_a = sb("w_out_a", [P, KD // 2, D], scope=s)
        with ExitStack() as s:
            raw = sb("raw", [P, RING, 2 * FF], scope=s)
        sb("raw_0_1", [P, 2, 2 * FF])
        x2T_hi = sb("x2T_hi", [P, 2, KD, P], F32R)
        x2T_lo = sb("x2T_lo", [P, 2, KD, P], F32R)
        sb("raw_4_5", [P, 2, 2 * FF])

        with ExitStack() as s:
            ext = sb("ext", [P, G, EXT], scope=s)
            with ExitStack() as s2:
                w_z_hi1 = sb("w_z_hi1", [P, KD // 2, PW], F32R, scope=s2)
            uT = sb("uT", [P, G, T], scope=s)
            gain = sb("gain", [P, D], scope=s)
            gain2 = sb("gain2", [P, D], scope=s)
            xn = sb("xn", [P, 2, D], scope=s)
            with ExitStack() as s2:
                w_z_hi0 = sb("w_z_hi0", [P, KD // 2, PW], F32R, scope=s2)
            h2T = sb("h2T", [P, 2, KD, P], scope=s)
            junk = sb("junk", [P, D], scope=s)
            with ExitStack() as s2:
                v_sb = sb("v_sb", [P, TT, SG], scope=s2)
                sumA = sb("sumA", [P, EXT], scope=s2)
                sumB = sb("sumB", [P, EXT], scope=s2)
                diff = sb("diff", [P, T], scope=s2)
                gated = sb("gated", [P, T], scope=s2)
            w_proj_sb = sb("w_proj_sb", [P, KP, D], scope=s)
            pT = sb("pT", [P, KP, T], scope=s)
            p_sb = sb("p_sb", [P, TT, PD], scope=s)
            chosen_row = sb("chosen_row", [P, TT, TOPK, E], scope=s)
            with ExitStack() as s2:
                w_pool_sb = sb("w_pool_sb", [P, G, P], scope=s2)
                sgu_w_sb = sb("sgu_w_sb", [P, G, P], scope=s2)
                wsT = sb("wsT", [P, G, P], scope=s2)
                sgu_bias = sb("sgu_bias", [P, G, P], scope=s2)
            rank = sb("rank", [P, TT, E], scope=s)
            depth = sb("depth", [P, TT, E], scope=s)
            first = sb("first", [P, TT, E], scope=s)
            over_cmp = sb("over_cmp", [P, OVER + 2, E], scope=s)
            chosen = sb("chosen", [P, TT, TOPK, E], scope=s)
            sb("rest_of_sgu_weights", [P, 4 * G * P - (3 * TT + OVER + 2 + TT * TOPK) * E], scope=s)
            ln_g = sb("ln_g", [P, SG], scope=s)
            ln_b = sb("ln_b", [P, SG], scope=s)
            state_sb = sb("state_sb", [P, PW], scope=s)
            scale4 = sb("scale4", [G, P], scope=s)
            scaleT = sb("scaleT", [P, G], scope=s)
            same_seq = sb("same_seq", [P, DB, DS], scope=s)
            block_w = sb("block_w", [P, G, NS], scope=s)
            rep = sb("rep", [P, NS], scope=s)
            head_fix = sb("head_fix", [P, G, LEAD], scope=s)
            new_cols = sb("new_cols", [P, G, NS], scope=s)
            pos_iota = sb("pos_iota", [P, LEAD], scope=s)
            pool_rows = sb("pool_rows", [P, PW], scope=s)
            pool_rows_s = sb("pool_rows_s", [P, PW], scope=s)
            stats = sb("stats", [P, G, 6], scope=s)
            mean_var = sb("mean_var", [P, TT, G, 2], scope=s)
            ln_var = sb("ln_var", [P, TT, G], scope=s)
            ln_rstd = sb("ln_rstd", [P, TT, G], scope=s)
            sq1 = sb("sq1", [P, TT], scope=s)
            var1 = sb("var1", [P, TT], scope=s)
            rstd1 = sb("rstd1", [P, TT], scope=s)
            sq2 = sb("sq2", [P, TT], scope=s)
            var2 = sb("var2", [P, TT], scope=s)
            rstd2 = sb("rstd2", [P, TT], scope=s)
            w_router_sb = sb("w_router_sb", [P, KD, E], scope=s)
            b_router_sb = sb("b_router_sb", [1, E], scope=s)
            ones = sb("ones", [P, P], scope=s)
            before = sb("before", [P, P], scope=s)
            logits = sb("logits", [P, TT, E], scope=s)
            top8 = sb("top8", [P, TT, 8], scope=s)
            top_i = sb("top_i", [P, TT, 8], U32, scope=s)
            top_f = sb("top_f", [P, TT, TOPK], scope=s)
            neg_max = sb("neg_max", [P, TT], scope=s)
            exps = sb("exps", [P, TT, TOPK], scope=s)
            exp_sum = sb("exp_sum", [P, TT], scope=s)
            exp_rcp = sb("exp_rcp", [P, TT], scope=s)
            expert_iota = sb("expert_iota", [P, E], scope=s)
            row_code = sb("row_code", [P, TT, TOPK], scope=s)
            mask = sb("mask", [P, TT, E], scope=s)
            count = sb("count", [P, E], scope=s)
            over = sb("over", [P, E], scope=s)
            over_end = sb("over_end", [P, E], scope=s)
            over_from = sb("over_from", [P, E], scope=s)

        assert KP * D + TT * PD + KP * T + TT * TOPK * E >= TT * SG + 2 * EXT + 2 * T

        with ExitStack() as s:
            w_hi = sb("w_hi", [P, SPLIT, 2 * FF], F32R, scope=s)
            w_lo = sb("w_lo", [P, SPLIT, 2 * FF], F32R, scope=s)
            lin = sb("lin", [P, FF], scope=s)
            aT_hi = sb("aT_hi", [P, KD, P], F32R, scope=s)
            aT_lo = sb("aT_lo", [P, KD, P], F32R, scope=s)
            y_rows = sb("y_rows", [P, D], scope=s)
            xT_hi = sb("xT_hi", [P, KD, P], F32R, scope=s)
            xT_lo = sb("xT_lo", [P, KD, P], F32R, scope=s)
            glu = sb("glu", [P, FF], scope=s)
            sig = sb("sig", [P, FF], scope=s)
            oh_up = sb("oh_up", [P, P], F32R, scope=s)
            oh_dn = sb("oh_dn", [P, P], F32R, scope=s)

        with ExitStack() as s:
            gate_lo = sb("gate_lo", [P, KD, D], F32R, scope=s)
            gate = sb("gate", [P, 2, D], scope=s)
            out_rows = sb("out_rows", [P, 2, D], scope=s)
            gain_f = sb("gain_f", [P, D], scope=s)
            sb("aT_and_y_rows", [P, 3, D], scope=s)
            gate_hi = [sb(f"gate_hi{i}", [P, 2, D], F32R, scope=s) for i in range(2)]
            sb("bias_picks", [P, 2, P], scope=s)
            gate_hi += [sb("gate_hi2", [P, 2, D], F32R, scope=s), gate_hi3]
            sq3 = sb("sq3", [P, TT], scope=s)
            var3 = sb("var3", [P, TT], scope=s)
            rstd3 = sb("rstd3", [P, TT], scope=s)
        w_z_hi = (w_z_hi0, w_z_hi1)
        w_z_halves = [slice(i * KD // 2, (i + 1) * KD // 2) for i in range(2)]
        HT = T // 2
        assert SEQ > HT
        STORES = 3 + DB
        YB = 2
        YK_SLOT = (4, 0)

        ps = ctx.enter_context(nc.psum_tensor("ps", [P, 8, 512], F32))

        START = [("xT", 0), ("v", 0), ("xT", 1), ("xT", 2), ("v", 1), ("xT", 3), ("xT", 4), ("v", 2), ("misc", 0), ("v", 3),
                 ("blockw", 0), ("v", 4)]
        assert TT == 5
        JOBS = [(name, "A" if name[0] in ("xT", "v") else "V") for name in START]
        JOBS += [(("z", g), "A") for g in range(G)] + [(("newpool", 0), "A")]
        for g in range(G):
            JOBS += [(("u", g), "A"), (("pool", g), "V"), (("gating", g), "V")]
        for t in range(TT + 2):
            if t < TT:
                JOBS.append((("out", t), "V"))
            if t == LAST:
                JOBS += [(("pT", i), "A") for i in range(TT)]
            if t == TT:
                JOBS.append((("ple", 0), "A"))
            if 0 <= t - 1 < TT:
                JOBS.append((("h2T", t - 1), "A"))
            if 0 <= t - 2 < TT:
                JOBS.append((("logits", t - 2), "V"))
        JOBS += [(("ple", 1), "A"), (("rank", 0), "V"), (("count", 0), "V"), (("slots", 0), "V")] + [(("ple", t), "A") for t in range(2, TT)]
        assert TT == 5 and (len(JOBS) - 1) % 4 != 3
        JOB = {name: n for n, (name, _) in enumerate(JOBS)}
        EMPTIED = {}
        for n, (name, who) in enumerate(JOBS):
            EMPTIED[name] = sum(w == who for _, w in JOBS[:n + 1])
        TOTAL = {who: sum(w == who for _, w in JOBS) for who in "AV"}

        s_job = sem("job_filled")
        s_emptied = {"A": sem("job_emptied_act"), "V": sem("job_emptied_dve")}

        def bank(name, b=0):
            return ps[:, 2 * (JOB[name] % 4) + b, :]

        def banks(name):
            n = 2 * (JOB[name] % 4)
            return ps[:, n:n + 2, :]

        def job_free(pe, name):
            n = JOB[name]
            if n >= 4:
                old, who = JOBS[n - 4]
                pe.wait_ge(s_emptied[who], EMPTIED[old])

        def job_filled(eng, name):
            eng.wait_ge(s_job, JOB[name] + 1)

        ld = {n: sem("ld_" + n) for n in (
            "gain w_v w_z w_u small pool_w state sgu ln w_out gain2 router bias ple p gain_f w_out2 w_out3".split())}
        s_x = [sem(f"ld_x_{t}") for t in range(TT)]
        s_ident = sem("ident_made")
        s_const = sem("constants_made")
        s_resid0 = sem("resid_tail_zeroed")
        s_sq = sem("squares_summed")
        s_var = sem("variances")
        s_rstd = sem("rstds")
        s_xn = sem("xn_ready")
        s_chain = sem("dve_chain")
        s_achain = sem("act_chain")
        s_pchain = sem("pool_chain")
        s_wpart = sem("mask_parts")
        s_lnv = sem("ln_variances")
        s_lnr = sem("ln_rstds")
        s_v = sem("v_normed")
        s_ext0 = sem("ext_zeroed")
        s_sum = sem("window_sums")
        s_diff = sem("diffs")
        s_mix = sem("mix_written")
        s_xrow = [sem(f"xn_rows_stored_{t}") for t in range(TT)]
        s_top = sem("tops")
        s_exp = sem("exps")
        s_mask = sem("masks")
        s_route = sem("routing_ready")
        s_bias_hi = sem("bias_hi")
        s_bias = sem("bias_table")
        s_out = sem("outputs_stored")

        ring = [sem(f"raw_landed_{i}") for i in range(RING)]
        s_hi = sem("chunk_hi")
        s_lo = {"V": sem("chunk_lo_dve"), "P": sem("chunk_lo_pool")}
        s_hused = sem("chunk_hi_used")
        s_lused = sem("chunk_lo_used")
        s_picks = sem("picks_ready")
        s_rowps = sem("slots_summed")
        s_rows = sem("row_numbers")
        s_gather = sem("x_rows_landed")
        s_xtp = sem("x_transposed")
        s_xhi = sem("xT_hi_ready")
        s_xlo = sem("xT_lo_ready")
        s_oh = sem("bias_picks_ready")
        s_glu = sem("glu_ready")
        s_lin = sem("lin_ready")
        s_sig = sem("sigmoid_ready")
        s_gs = sem("swish_ready")
        s_act = sem("activation_ready")
        s_atp = sem("activation_transposed")
        s_ahi = sem("aT_hi_ready")
        s_alo = sem("aT_lo_ready")
        s_y = sem("y_rows_ready")
        s_scat = sem("y_rows_stored")
        s_xzero = sem("x_rows_zeroed")
        s_xh = sem("xT_high_parts")
        s_xl = sem("xT_low_parts")
        s_wzh = sem("w_z_high_parts")
        s_wzl = sem("w_z_low_parts")
        s_wuh = sem("w_u_high_part")
        s_wul = sem("w_u_low_part")

        s_yk = [[sem(f"expert_rows_landed_{i}_{h}") for h in range(2)] for i in range(YB)]
        s_comb = sem("moe_added")
        s_x2tp = sem("x2_transposed")
        s_x2h = sem("x2T_hi_ready")
        s_x2l = sem("x2T_lo_ready")
        s_ghi = sem("gate_weights_hi")
        s_glo = sem("gate_weights_lo")
        s_gmm = sem("gate_done")
        s_gate = sem("gate_sigmoid")
        s_x3 = sem("x3_ready")
        s_sq3 = sem("squares3")
        s_var3 = sem("var3_ready")
        s_rstd3 = sem("rstd3_ready")
        s_orow = sem("out_rows_ready")
        s_ost = [sem("out_rows_stored_even"), sem("out_rows_stored_odd")]
        s_tchain = sem("tail_chain")

        gu = ps[:, 0:4, :].rearrange("p a b -> p (a b)")
        dn = ps[:, 4:6, :].rearrange("p a b -> p (a b)")
        tp = ps[:, 6:8, :].rearrange("p a b -> p (a b)")
        slot_sum = ps[:, 4, 0:1]
        LOS = {"V": [sum(c % STEP_CHUNKS not in POOL_LO for c in range(s)) for s in range(2 * STEP_CHUNKS + 1)],
               "P": [sum(c % STEP_CHUNKS in POOL_LO for c in range(s)) for s in range(2 * STEP_CHUNKS + 1)]}
        PER = {"V": STEP_CHUNKS - len(POOL_LO), "P": len(POOL_LO)}

        def lo_by(s):
            return "P" if s % STEP_CHUNKS in POOL_LO else "V"

        def wait_lo(eng, J, s):
            who = lo_by(s)
            eng.wait_ge(s_lo[who], PER[who] * J + LOS[who][s] + 1)

        def wait_hi(eng, J, s):
            eng.wait_ge(s_hi, STEP_CHUNKS * J + s + 1)

        def wait_split_used(eng, used, J, s):
            if not (isinstance(J, int) and STEP_CHUNKS * J + s < SPLIT):
                eng.wait_ge(used, STEP_CHUNKS * J + s - SPLIT + 1)

        def wait_landed(eng, J, s):
            eng.wait_ge(ring[s % RING], 32 * J + 16 * (s // RING) + 16)

        def tail_gate(act, t):
            act.wait_ge(s_gmm, t + 1)
            if t >= 2:
                act.wait_ge(s_x3, t - 1)
            act.activation(gate[:, t % 2, :], ps[:, 2 * (t % 2):2 * (t % 2) + 2, :].rearrange("p a n -> p (a n)"),
                           ACT.Sigmoid).then_inc(s_gate, 1)
            act.wait_ge(s_x3, t + 1)
            if t >= 1:
                act.wait_ge(s_sq3, t)
            act.activation(junk_t[:], resid[:, t, :], ACT.Square, accum_out=sq3[:, t:t + 1]).then_inc(s_sq3, 1)

        def gate_hi_products(pe, t):
            pe.wait_ge(s_x2h, t + 1)
            pe.wait_ge(s_ghi, DN_CHUNKS)
            pe.wait_ge(s_glo, DN_CHUNKS)
            if t >= 2:
                pe.wait_ge(s_gate, t - 1)
            for b in range(2):
                cols = slice(b * 512, (b + 1) * 512)
                for k in range(KD):
                    pe.matmul(ps[:, 2 * (t % 2) + b, :], x2T_hi[:, t % 2, k, :], gate_hi[k // 2][:, k % 2, cols],
                              start=(k == 0), stop=False, skip_group_check=True)
                    pe.matmul(ps[:, 2 * (t % 2) + b, :], x2T_hi[:, t % 2, k, :], gate_lo[:, k, cols],
                              start=False, stop=False, skip_group_check=True)

        def gate_low_products(pe, t):
            pe.wait_ge(s_x2l, t + 1)
            for b in range(2):
                for k in range(KD):
                    mm = pe.matmul(ps[:, 2 * (t % 2) + b, :], x2T_lo[:, t % 2, k, :],
                                   gate_hi[k // 2][:, k % 2, b * 512:(b + 1) * 512], start=False, stop=(k == KD - 1),
                                   skip_group_check=True)
            mm.then_inc(s_gmm, 1)

        block = ctx.enter_context(nc.Block())

        @block.sync
        def _(sp):
            def load(dst, src, name):
                sp.dma_start(dst, src).then_inc(ld[name], 16)

            w_in_v = w_in.rearrange("a (k p) n -> p (a k) n", p=P)

            def load_x(t):
                sp.dma_start(resid[:, t, :], x_prompt[0, t * P:(t + 1) * P, :]).then_inc(s_x[t], 16)

            load_x(0)
            load(w_v_sb[:, 0:KD // 2, :], w_in_v[:, 0:KD // 2, PW + SG:], "w_v")
            load_x(1)
            load(w_v_sb[:, KD // 2:, :], w_in_v[:, KD // 2:, PW + SG:], "w_v")
            load_x(2)
            load_x(3)
            sp.wait_ge(s_resid0, 1)
            sp.dma_start(resid[0:NS, LAST, :], x_sample.rearrange("b s d -> (b s) d")).then_inc(s_x[LAST], 16)
            load(sgu_w_sb[:], sgu_w[0].rearrange("h i j -> i h j"), "sgu")
            load(state_sb[0:DB * PB, :], state_pool[0].rearrange("b r c -> (b r) c"), "state")
            load(scale4[:], pool_scale[0], "state")
            load(ln_g[:], sgu_ln_g.rearrange("a h i -> (a h i)").partition_broadcast(P), "ln")
            load(ln_b[:], sgu_ln_b.rearrange("a h i -> (a h i)").partition_broadcast(P), "ln")
            for k in range(0, KD, 4):
                load(w_z_sb[:, k:k + 4, :], w_in_v[:, k:k + 4, 0:PW], "w_z")
            load(w_pool_sb[:], w_pool[0].rearrange("g c d -> c g d"), "pool_w")
            load(sgu_bias[:].rearrange("p h i -> p (h i)"), sgu_b.rearrange("a h i -> (a h i)").partition_broadcast(P), "small")
            load(gain2[:], norm_ffn[0].partition_broadcast(P), "gain2")
            load(w_router_sb[:], w_router[0].rearrange("(k p) e -> p k e", p=P), "router")
            load(b_router_sb[:], b_router, "router")
            for k in range(0, KD, 4):
                load(w_u_sb[:, k:k + 4, :], w_in_v[:, k:k + 4, PW:PW + SG], "w_u")
            sp.dma_start(new_pool_sample[0, :, 0:PB - DS, :], state_pool[0, :, DS:PB, :]).then_inc(s_out, 16)
            w_out_v = w_out.rearrange("a (i k p) n -> p (a i) k n", p=P, k=KD // 2)
            sp.wait_ge(s_job, JOB[("z", G - 1)] + 1)
            load(w_out_a[:], w_out_v[:, 0], "w_out")
            sp.wait_ge(s_job, JOB[("u", G - 1)] + 1)
            load(w_out_b[:, 0:KD // 4, :], w_out_v[:, 1, 0:KD // 4, :], "w_out2")
            load(w_out_b[:, KD // 4:, :], w_out_v[:, 1, KD // 4:, :], "w_out3")

            def raw_free(J, s):
                if isinstance(J, int):
                    sp.wait_ge(s_job, JOB[("u", G - 1) if s in (RING - 2, RING - 1) else ("out", LAST)] + 1)
                    if STEP_CHUNKS * J + s >= RING:
                        wait_hi(sp, J, s - RING)
                        wait_lo(sp, J, s - RING)
                    return
                who = lo_by(s - RING)
                hi = sp.to_reg(J * STEP_CHUNKS + (s - RING + 1))
                lo = sp.to_reg(J * PER[who] + (LOS[who][s - RING] + 1))
                sp.wait_ge(s_job, JOB[("out", LAST)] + 1)
                sp.wait_ge(s_hi, hi)
                sp.wait_ge(s_lo[who], lo)

            def load_up(J, s, e, c):
                raw_free(J, s)
                sp.dma_start(raw[:, s % RING, :], up_dram[bass.ds(e * UP_CHUNKS + c, 1), :, :].rearrange(
                    "a p n -> p (a n)")).then_inc(ring[s % RING], 16)

            def load_dn(J, s, e, c):
                raw_free(J, s)
                sp.dma_start(raw[:, s % RING, :].rearrange("p (j n) -> p j n", j=2),
                             dn_dram[bass.ds(e * DN_CHUNKS + c, 1), :, :, :].rearrange(
                                 "a p j n -> p (a j) n")).then_inc(ring[s % RING], 16)

            def step(J, e_up, e_dn):
                for c in range(UP_CHUNKS):
                    load_up(J, UP_CHUNKS + c, e_up, c)
                for c in range(DN_CHUNKS):
                    load_dn(J, 2 * UP_CHUNKS + c, e_dn, c)

            for c in range(RING - 2, RING):
                load_up(0, c, 0, c)
            sp.wait_ge(s_mix, 2 * G)
            sp.wait_ge(s_out, 16 * STORES)
            load(w_proj_sb[:], w_ple_proj.rearrange("a (k p) n -> p (a k) n", p=P), "ple")
            load(p_sb[:, 0:LAST, :], p_prompt[0, 0].rearrange("(t p) n -> p t n", p=P), "p")
            load(p_sb[0:NS, LAST, :], p_sample.rearrange("a b s n -> (a b s) n"), "p")
            for t in range(TT):
                sp.wait_ge(s_xn, TT + t + 1)
                sp.dma_start(xn_dram[t * P:t * P + NT[t], :], xn[0:NT[t], t % 2, :]).then_inc(s_xrow[t], 16)
            for c in (*range(RING - 2), *range(RING, UP_CHUNKS)):
                if c == FIRST_GATHER:
                    sp.wait_ge(s_gather, 16)
                load_up(0, c, 0, c)
            with sp.Fori(0, E - 1) as J:
                step(J, J + 1, J)
            sp.wait_ge(s_route, 1)
            n_over = sp.value_load(over_i[0:1, 0:1], min_val=0, max_val=OVER)
            with sp.If(n_over > 0):
                with sp.Fori(0, OVER) as b:
                    with sp.If(b < n_over):
                        e_up = sp.value_load(block_expert_i[0:1, bass.ds(b + E, 1)], min_val=0, max_val=E - 1)
                        e_dn = sp.value_load(block_expert_i[0:1, bass.ds(b + (E - 1), 1)], min_val=0, max_val=E - 1)
                        step(b + (E - 1), e_up, e_dn)
            e_dn = sp.value_load(block_expert_i[0:1, bass.ds(n_over + (E - 1), 1)], min_val=0, max_val=E - 1)
            for c in range(DN_CHUNKS):
                load_dn(n_over + (E - 1), UP_CHUNKS + c, e_dn, c)
            J = n_over + (E - 1)
            gate_v = w_ple_gate.rearrange("a (c j p) n -> (a c) p j n", p=P, j=2)
            for c in range(DN_CHUNKS):
                raw_free(J, STEP_CHUNKS + c)
                sp.dma_start(raw[:, c, :].rearrange("p (j n) -> p j n", j=2), gate_v[c]).then_inc(ring[c], 16)
            sp.wait_ge(s_atp, n_over + E)
            sp.dma_start(gain_f[:], norm_final.partition_broadcast(P)).then_inc(ld["gain_f"], 16)
            sp.wait_ge(s_scat, 16 * n_over + 16 * E)
            y4 = y4_dram.rearrange("(t k) d -> t (k d)", k=TOPK)
            for t in range(TT):
                if t == 1:
                    sp.wait_ge(s_glo, 2)
                if t >= YB:
                    sp.wait_ge(s_comb, t - YB + 1)
                i = YK_SLOT[t % YB]
                for h in range(2):
                    sp.dma_start(raw[0:NT[t], i + h, :], y4[t * P:t * P + NT[t], h * 2 * D:(h + 1) * 2 * D]).then_inc(s_yk[t % YB][h], 16)
            for t in range(TT):
                sp.wait_ge(s_orow, t + 1)
                dst = y_prompt[0, t * P:(t + 1) * P, :] if t < LAST else y_sample.rearrange("b s d -> (b s) d")
                sp.dma_start(dst, out_rows[0:NT[t], t % 2, :]).then_inc(s_ost[t % 2], 16)
            sp.wait_ge(s_ost[0], 16 * ((TT + 1) // 2))
            sp.wait_ge(s_ost[1], 16 * (TT // 2))
            sp.wait_ge(s_out, 16 * STORES)

        @block.gpsimd
        def _(pool):
            chain = [0]

            def link(ins):
                chain[0] += 1
                ins.then_inc(s_pchain, 1)
                pool.wait_ge(s_pchain, chain[0])

            pool.memset(resid[:, LAST, :], 0.0).then_inc(s_resid0, 1)
            pool.memset(half_neg[:], -0.5).then_inc(s_const, 1)
            link(pool.memset(ident[:], 0.0))
            pool.affine_select(out=ident[:], in_=ident[:], compare_op=ALU.not_equal, fill=1.0, base=0,
                               pattern=[[-1, P]], channel_multiplier=1).then_inc(s_ident, 1)
            pool.wait_ge(s_const, 1)
            for t in range(TT):
                pool.wait_ge(s_var, t + 1)
                pool.tensor_tensor(rstd1[:, t:t + 1], var1[:, t:t + 1], half_neg[:, 0:1], ALU.pow).then_inc(s_rstd, 1)
            pool.wait_ge(ld["sgu"], 16)
            pool.affine_select(out=sgu_w_sb[:], in_=sgu_w_sb[:], compare_op=ALU.is_ge, fill=0.0, base=0,
                               pattern=[[0, G], [-1, P]], channel_multiplier=1).then_inc(s_wpart, 1)
            link(pool.memset(same_seq[:], 1.0))
            link(pool.affine_select(out=same_seq[:], in_=same_seq[:], compare_op=ALU.is_ge, fill=0.0, base=0,
                                    pattern=[[-DS, DB], [0, DS]], channel_multiplier=1))
            pool.affine_select(out=same_seq[:], in_=same_seq[:], compare_op=ALU.is_ge, fill=0.0, base=DS - 1,
                               pattern=[[DS, DB], [0, DS]], channel_multiplier=-1).then_inc(s_wpart, 1)
            pool.memset(ext[:, :, 0:LEAD], 0.0).then_inc(s_ext0, 1)
            pool.memset(ext[:, :, LEAD + SEQ:], 0.0).then_inc(s_ext0, 1)
            link(pool.iota(pos_iota[:], pattern=[[1, LEAD]], base=1, channel_multiplier=0,
                           allow_small_or_imprecise_dtypes=True))
            for g, w in enumerate(WINDOWS):
                pool.tensor_scalar(head_fix[:, g, :], pos_iota[:], float(w), None, ALU.min).then_inc(s_const, 1)
            pool.memset(ones[:], 1.0).then_inc(s_const, 1)
            link(pool.memset(before[:], 1.0))
            pool.affine_select(out=before[:], in_=before[:], compare_op=ALU.is_gt, fill=0.0, base=0,
                               pattern=[[1, P]], channel_multiplier=-1).then_inc(s_const, 1)
            pool.iota(expert_iota[:], pattern=[[1, E]], base=0, channel_multiplier=0,
                      allow_small_or_imprecise_dtypes=True).then_inc(s_const, 1)
            pool.iota(slot1[:], pattern=[[1, P]], base=1, channel_multiplier=0,
                      allow_small_or_imprecise_dtypes=True).then_inc(s_const, 1)
            pool.iota(block_iota[:], pattern=[[1, NBLK]], base=0, channel_multiplier=0,
                      allow_small_or_imprecise_dtypes=True).then_inc(s_const, 1)
            pool.iota(row_code[:], pattern=[[TOPK * P, TT], [1, TOPK]], base=-NO_ROW, channel_multiplier=TOPK,
                      allow_small_or_imprecise_dtypes=True).then_inc(s_const, 1)
            pool.memset(mask[:], 0.0).then_inc(s_const, 1)
            pool.memset(cur_block[:], 0.0).then_inc(s_const, 1)
            link(pool.iota(bias_row[:], pattern=[[0, 1]], base=0, channel_multiplier=1,
                           allow_small_or_imprecise_dtypes=True))
            link(pool.tensor_scalar(bias_row[E:2 * E, :], bias_row[E:2 * E, :], float(E), None, ALU.subtract))
            pool.tensor_scalar(bias_row[2 * E:P, :], bias_row[2 * E:P, :], 1000.0, None, ALU.add).then_inc(s_const, 1)
            pool.wait_ge(s_const, 14)
            for t in range(TT):
                pool.wait_ge(s_lnv, t + 1)
                pool.tensor_tensor(ln_rstd[0:NT[t], t, :], ln_var[0:NT[t], t, :], half_neg[0:NT[t], 0:G],
                                   ALU.pow).then_inc(s_lnr, 1)
            pool.wait_ge(s_lnr, TT)
            pool.wait_ge(s_ext0, 2)
            for g in range(G):
                job_emptied = EMPTIED[("z", g)]
                pool.wait_ge(s_emptied["A"], job_emptied)
                pool.wait_ge(s_emptied["V"], EMPTIED[("misc", 0)])
                src = ext[:, g, :]
                if g >= 1:
                    pool.wait_ge(s_diff, g)
                for i in range(g + 1):
                    dst = (sumA, sumB)[(g - i) % 2]
                    sh = 1 << i
                    lo = (2 << i) - 1
                    ins = pool.tensor_tensor(dst[:, lo:EXT], src[:, lo:EXT], src[:, lo - sh:EXT - sh], ALU.add)
                    if i < g:
                        link(ins)
                    else:
                        ins.then_inc(s_sum, 1)
                    src = dst
            pool.wait_ge(s_job, JOB[("u", G - 1)] + 1)
            pool.memset(x_rows[:], 0.0).then_inc(s_xzero, 1)
            pool.wait_ge(s_xzero, 1)
            pool.wait_ge(s_sum, G)
            pool.memset(bias_hl[2 * E:P, :].bitcast(F32), 0.0).then_inc(s_bias, 1)
            pool.wait_ge(s_bias, 1)
            pool.wait_ge(s_sum, G)
            for t in range(TT):
                pool.wait_ge(s_var, TT + t + 1)
                pool.tensor_tensor(rstd2[:, t:t + 1], var2[:, t:t + 1], half_neg[:, 0:1], ALU.pow).then_inc(s_rstd, 1)
            last_token = pool.to_reg(T - 1)
            last_row = pool.to_reg(T * TOPK - 1)

            def gather(u):
                found, used = (u + 1, u) if isinstance(u, int) else (pool.to_reg(u + 1), pool.to_reg(u))
                pool.wait_ge(s_xzero, 1)
                for t in range(TT):
                    pool.wait_ge(s_xrow[t], 16)
                pool.wait_ge(s_rows, found)
                if not (isinstance(u, int) and u == 0):
                    pool.wait_ge(s_xtp, used)
                pool.indirect_dma_start(x_rows[:], None, xn_dram[:, :],
                                        bass.IndirectOffsetOnAxis(ap=token_of[:, 0:1], axis=0),
                                        bounds_check=last_token, oob_is_err=False).then_inc(s_gather, 16)

            def scatter(u, col):
                ready = u + 1 if isinstance(u, int) else pool.to_reg(u + 1)
                pool.wait_ge(s_route, 1)
                pool.wait_ge(s_y, ready)
                pool.indirect_dma_start(y4_dram[:, :], bass.IndirectOffsetOnAxis(ap=rows[:, col:col + 1], axis=0),
                                        y_rows[:], None,
                                        bounds_check=last_row, oob_is_err=False).then_inc(s_scat, 16)

            def lo_part(J, s):
                wait_split_used(pool, s_lused, J, s)
                wait_hi(pool, J, s)
                pool.tensor_tensor(w_lo[:, s % SPLIT, :], raw[:, s % RING, :], w_hi[:, s % SPLIT, :].bitcast(F32),
                                   ALU.subtract).then_inc(s_lo["P"], 1)

            def swish(u):
                pool.wait_ge(s_sig, u + 1)
                pool.tensor_tensor(sig[:], glu[:], sig[:], ALU.mult).then_inc(s_gs, 1)

            def step(J, scatters=True):
                for x in range(STEP_CHUNKS):
                    s = UP_CHUNKS + x
                    if x == 7:
                        gather(J + 2)
                        if scatters:
                            scatter(J - 1, 3)
                    if lo_by(s) == "P":
                        lo_part(J, s)
                swish(J + 1)

            gather(0)
            gather(1)
            for s in range(UP_CHUNKS):
                if lo_by(s) == "P":
                    lo_part(0, s)
            swish(0)
            step(0, scatters=False)
            step(1)
            with pool.Fori(2, E - 1) as J:
                step(J)
            n_over = pool.value_load(over_i[0:1, 0:1], min_val=0, max_val=OVER)
            with pool.If(n_over > 0):
                with pool.Fori(0, OVER) as b:
                    with pool.If(b < n_over):
                        step(b + (E - 1))
            for x in range(DN_CHUNKS):
                if lo_by(UP_CHUNKS + x) == "P":
                    lo_part(n_over + (E - 1), UP_CHUNKS + x)
            scatter(n_over + (E - 2), 2)
            scatter(n_over + (E - 1), 1)
            for t in range(TT):
                pool.wait_ge(s_var3, t + 1)
                pool.tensor_tensor(rstd3[:, t:t + 1], var3[:, t:t + 1], half_neg[:, 0:1], ALU.pow).then_inc(s_rstd3, 1)

        @block.scalar
        def _(act):
            act.dma_start(gain[:], norm_mix[0].partition_broadcast(P)).then_inc(ld["gain"], 16)

            def square1(t):
                act.wait_ge(s_x[t], 16)
                if t == LAST:
                    act.wait_ge(s_resid0, 1)
                if t >= 1:
                    act.wait_ge(s_sq, t)
                act.activation(junk[:], resid[:, t, :], ACT.Square, accum_out=sq1[:, t:t + 1]).then_inc(s_sq, 1)

            square1(0)
            for what, t in START:
                if what == "xT":
                    job_filled(act, ("xT", t))
                    act.activation(xT[:, :, t * P:(t + 1) * P],
                                   banks(("xT", t)).rearrange("p a (b n) -> p (a b) n", n=P),
                                   ACT.Copy).then_inc(s_emptied["A"], 1)
                    for ts in {0: (1, 2, 3), 1: (4,)}.get(t, ()):
                        square1(ts)
                elif what == "v":
                    job_filled(act, ("v", t))
                    act.activation(v_sb[0:NT[t], t, :], bank(("v", t))[0:NT[t], :], ACT.Gelu).then_inc(s_emptied["A"], 1)
                if (what, t) == ("xT", LAST):
                    act.wait_ge(ld["w_z"], 32)
                    for i, ks in enumerate(w_z_halves):
                        act.activation(w_z_hi[i][:], w_z_sb[:, ks, :], ACT.Copy).then_inc(s_wzh, 1)
                    for i in range(TT):
                        act.wait_ge(s_emptied["A"], EMPTIED[("xT", i)])
                        act.activation(xTh[:, :, i * P:i * P + NT[i]], xT[:, :, i * P:i * P + NT[i]], ACT.Copy).then_inc(s_xh, 1)
            act.wait_ge(ld["w_u"], 32)
            act.activation(w_u_hi[:], w_u_sb[:], ACT.Copy).then_inc(s_wuh, 1)
            act.wait_ge(s_ext0, 2)
            act.wait_ge(s_emptied["V"], EMPTIED[("misc", 0)])
            for g in range(G):
                name = ("z", g)
                job_filled(act, name)
                new = bank(name, 1)[:, SEQ - HT:HT]
                act.activation(ext[:, g, LEAD:LEAD + HT], bank(name)[:, 0:HT], ACT.Copy)
                act.activation(ext[:, g, LEAD + HT:LEAD + SEQ], bank(name, 1)[:, 0:SEQ - HT], ACT.Copy)
                act.activation(new_cols[:, g, :], new, ACT.Copy)
                act.activation(ext[:, g, LEAD + SEQ:].rearrange("p (b s) -> p b s", b=DB)[:, :, LEAD:],
                               new.rearrange("p (b s) -> p b s", b=DB), ACT.Copy).then_inc(s_emptied["A"], 1)
            job_filled(act, ("newpool", 0))
            act.activation(pool_rows[0:PB, :], bank(("newpool", 0))[0:PB, :], ACT.Copy).then_inc(s_achain, 1)
            act.activation(pool_rows_s[0:NS, :], bank(("newpool", 0), 1)[0:NS, :], ACT.Copy).then_inc(s_emptied["A"], 1)
            act.wait_ge(s_achain, 1)
            act.dma_start(new_pool_prompt[0, 0], pool_rows[0:PB, :]).then_inc(s_out, 16)
            act.wait_ge(s_emptied["A"], EMPTIED[("newpool", 0)])
            for b in range(DB):
                act.dma_start(new_pool_sample[0, b, PB - DS:PB, :], pool_rows_s[b * DS:(b + 1) * DS, :]).then_inc(s_out, 16)
            for g in range(G):
                name = ("u", g)
                job_filled(act, name)
                act.activation(uT[:, g, :].rearrange("p (b n) -> p b n", b=2), banks(name)[:, :, 0:HT],
                               ACT.Gelu).then_inc(s_emptied["A"], 1)
            act.wait_ge(s_v, TT)
            act.dma_start(new_sgu_v.rearrange("a b s c -> (a b s) c"), v_sb[0:NS, LAST, :]).then_inc(s_out, 16)
            act.wait_ge(s_mix, 2 * G)
            act.wait_ge(s_out, 16 * STORES)
            for i in range(2):
                act.dma_start(bias_raw[i * E:(i + 1) * E, 0:2 * FF], b_up[0]).then_inc(ld["bias"], 16)
                act.dma_start(bias_raw[i * E:(i + 1) * E, 2 * FF:], b_down[0]).then_inc(ld["bias"], 16)

            def square2(t):
                act.wait_ge(s_emptied["V"], EMPTIED[("out", t)])
                act.wait_ge(s_sq, TT + t)
                act.activation(junk[:], resid[:, t, :], ACT.Square, accum_out=sq2[:, t:t + 1]).then_inc(s_sq, 1)

            def bias_high():
                act.wait_ge(ld["bias"], 64)
                act.activation(bias_hl[0:2 * E, :], bias_raw[0:2 * E, :], ACT.Copy).then_inc(s_bias_hi, 1)

            def p_transposed(t):
                job_filled(act, ("pT", t))
                n = NT[t]
                act.activation(pT[:, :, t * P:t * P + n],
                               bank(("pT", t))[:, 0:KP * P].rearrange("p (k n) -> p k n", n=P)[:, :, 0:n],
                               ACT.Copy).then_inc(s_emptied["A"], 1)

            def ple_out(t):
                job_filled(act, ("ple", t))
                act.activation(ple[0:NT[t], t, :], banks(("ple", t))[0:NT[t]].rearrange("p a n -> p (a n)"),
                               ACT.Copy).then_inc(s_emptied["A"], 1)

            square2(0)
            for t in range(TT):
                if t + 1 < TT:
                    square2(t + 1)
                if t == 1:
                    bias_high()
                if t == LAST - 1:
                    for i in range(TT):
                        p_transposed(i)
                if t == LAST:
                    act.wait_ge(s_bias, 2)
                    ple_out(0)
                if t >= 2:
                    act.wait_ge(s_job, JOB[("logits", t - 2)] + 1)
                job_filled(act, ("h2T", t))
                act.activation(h2T[:, t % 2, :, :], banks(("h2T", t)).rearrange("p a (b n) -> p (a b) n", n=P),
                               ACT.Copy).then_inc(s_emptied["A"], 1)

            def hi_part(J, s):
                wait_landed(act, J, s)
                wait_split_used(act, s_hused, J, s)
                if not (isinstance(J, int) and STEP_CHUNKS * J + s < SPLIT):
                    wait_lo(act, J, s - SPLIT)
                act.activation(w_hi[:, s % SPLIT, :], raw[:, s % RING, :], ACT.Copy).then_inc(s_hi, 1)

            for t in range(TT):
                act.wait_ge(s_xrow[t], 16)
            act.wait_ge(s_job, JOB[("logits", LAST)] + 1)
            hi_part(0, 0)
            hi_part(0, 1)
            ple_out(1)
            for t in range(TT):
                act.wait_ge(s_top, t + 1)
                act.activation(exps[:, t, :], top8[:, t, 0:TOPK], ACT.Exp, bias=neg_max[:, t:t + 1],
                               accum_out=exp_sum[:, t:t + 1]).then_inc(s_exp, 1)
            hi_part(0, 2)
            ple_out(2)
            ple_out(3)

            def xT_high(u):
                act.wait_ge(s_xtp, u + 1)
                act.activation(xT_hi[:].rearrange("p k n -> p (k n)"), tp, ACT.Copy).then_inc(s_xhi, 1)

            def aT_high(u):
                act.wait_ge(s_atp, u + 1)
                act.activation(aT_hi[:].rearrange("p k n -> p (k n)"), tp, ACT.Copy).then_inc(s_ahi, 1)

            def sigmoid(u):
                act.wait_ge(s_glu, u + 1)
                act.activation(sig[:], glu[:], ACT.Sigmoid, scale=ALPHA).then_inc(s_sig, 1)

            def y_out(u, chunks):
                act.wait_ge(s_lused, chunks)
                if not (isinstance(u, int) and u == 0):
                    act.wait_ge(s_scat, 16 * u)
                act.activation(y_rows[:], dn, ACT.Copy).then_inc(s_y, 1)

            def step(J, first=False):
                for x in range(STEP_CHUNKS):
                    hi_part(J, UP_CHUNKS + x)
                    if x == 0 and first:
                        sigmoid(0)
                    if x == 2 and not first:
                        y_out(J - 1, STEP_CHUNKS * J + UP_CHUNKS)
                    if x == 4:
                        aT_high(J)
                    if x == 11:
                        sigmoid(J + 1)
                xT_high(J + 2)

            act.wait_ge(s_route, 1)
            xT_high(0)
            ple_out(LAST)
            for s in range(3, UP_CHUNKS):
                hi_part(0, s)
            act.wait_ge(s_lused, UP_CHUNKS)
            xT_high(1)
            step(0, first=True)
            step(1)
            with act.Fori(2, E - 1) as J:
                step(J)
            n_over = act.value_load(over_i[0:1, 0:1], min_val=0, max_val=OVER)
            with act.If(n_over > 0):
                with act.Fori(0, OVER) as b:
                    with act.If(b < n_over):
                        step(b + (E - 1))
            J = n_over + (E - 1)

            def gate_high(c):
                wait_landed(act, J, STEP_CHUNKS + c)
                act.activation(gate_hi[c][:].rearrange("p j n -> p (j n)"), raw[:, c, :], ACT.Copy).then_inc(s_ghi, 1)

            hi_part(J, UP_CHUNKS)
            hi_part(J, UP_CHUNKS + 1)
            act.wait_ge(s_lused, J * STEP_CHUNKS + UP_CHUNKS)
            aT_high(J)
            y_out(n_over + (E - 2), J * STEP_CHUNKS + UP_CHUNKS)
            hi_part(J, UP_CHUNKS + 2)
            hi_part(J, UP_CHUNKS + 3)
            act.wait_ge(s_act, n_over + E)
            act.wait_ge(s_xlo, n_over + (E + 1))
            gate_high(0)
            gate_high(1)
            y_out(J, J * STEP_CHUNKS + STEP_CHUNKS)
            gate_high(2)
            gate_high(3)

            act.wait_ge(s_glo, DN_CHUNKS)
            for t in range(TT):
                act.wait_ge(s_x2tp, t + 1)
                if t >= 2:
                    act.wait_ge(s_gmm, t - 1)
                act.activation(x2T_hi[:, t % 2, :, :].rearrange("p k n -> p (k n)"), ps[:, 4 + 2 * (t % 2):6 + 2 * (t % 2), :].rearrange("p a n -> p (a n)"),
                               ACT.Copy).then_inc(s_x2h, 1)
                if t >= 1:
                    tail_gate(act, t - 1)
            tail_gate(act, LAST)

        @block.tensor
        def _(pe):
            pe.wait_ge(s_ident, 1)

            def transposes(name, src):
                job_free(pe, name)
                for k in range(KD):
                    mm = pe.transpose(bank(name, k // 4)[:, (k % 4) * P:(k % 4 + 1) * P], src[:, k * P:(k + 1) * P], ident[:])
                mm.then_inc(s_job, 1)

            def project_v(t):
                name = ("v", t)
                job_free(pe, name)
                pe.wait_ge(s_emptied["A"], EMPTIED[("xT", t)])
                pe.wait_ge(ld["w_v"], 32)
                for k in range(KD):
                    mm = pe.matmul(bank(name), xT[:, k, t * P:(t + 1) * P], w_v_sb[:, k, :], start=(k == 0), stop=(k == KD - 1))
                mm.then_inc(s_job, 1)

            def misc():
                name = ("misc", 0)
                job_free(pe, name)
                pe.wait_ge(s_wpart, 1)
                pe.wait_ge(ld["state"], 32)
                for h in range(G):
                    pe.transpose(bank(name)[:, h * P:(h + 1) * P], sgu_w_sb[:, h, :], ident[:])
                n = DB * PB
                for g in range(G):
                    pe.transpose(bank(name, 1)[:, g * n:(g + 1) * n], state_sb[0:n, g * P:(g + 1) * P], ident[0:n, 0:n])
                pe.transpose(bank(name, 1)[:, G * n:G * n + G], scale4[:], ident[0:G, 0:G]).then_inc(s_job, 1)

            def block_weights():
                name = ("blockw", 0)
                job_free(pe, name)
                pe.wait_ge(s_chain, 1)
                pe.wait_ge(s_emptied["V"], EMPTIED[("misc", 0)])
                for h in range(G):
                    mm = pe.matmul(bank(name)[0:NS, h * DS:(h + 1) * DS], rep[0:DS, :], wsT[0:DS, h, 0:DS], start=True, stop=True)
                mm.then_inc(s_job, 1)

            for what, t in START:
                if what == "xT":
                    pe.wait_ge(s_xn, t + 1)
                    transposes(("xT", t), xn[:, t % 2, :])
                elif what == "v":
                    project_v(t)
                elif what == "misc":
                    misc()
                else:
                    block_weights()

            def project(name, w_hi_of, w_lo, g, x_low):
                job_free(pe, name)
                cols = slice(g * P, (g + 1) * P)
                for k in range(KD):
                    for b in range(2):
                        half = slice(b * HT, (b + 1) * HT)
                        pe.matmul(bank(name, b)[:, 0:HT], w_hi_of(k)[:, cols], xTh[:, k, half], start=(k == 0), stop=False,
                                  skip_group_check=True)
                        pe.matmul(bank(name, b)[:, 0:HT], w_lo[:, k, cols], xTh[:, k, half], start=False, stop=False,
                                  skip_group_check=True)
                for k in range(KD):
                    if x_low:
                        pe.wait_ge(s_xl, k + 1)
                    for b in range(2):
                        half = slice(b * HT, (b + 1) * HT)
                        mm = pe.matmul(bank(name, b)[:, 0:HT], w_hi_of(k)[:, cols], xTl[:, k, half], start=False,
                                       stop=(k == KD - 1), skip_group_check=True)
                mm.then_inc(s_job, 1)

            pe.wait_ge(s_wzh, 2)
            pe.wait_ge(s_wzl, 2)
            pe.wait_ge(s_xh, TT)
            for g in range(G):
                project(("z", g), lambda k: w_z_hi[k // (KD // 2)][:, k % (KD // 2)], w_z_lo, g, x_low=(g == 0))
            name = ("newpool", 0)
            job_free(pe, name)
            pe.wait_ge(s_emptied["A"], EMPTIED[("z", G - 1)])
            for g in range(G):
                pe.transpose(bank(name)[0:PB, g * P:(g + 1) * P], ext[:, g, LEAD + SEQ - PB:LEAD + SEQ], ident[:])
            for g in range(G):
                mm = pe.transpose(bank(name, 1)[0:NS, g * P:(g + 1) * P], new_cols[:, g, :], ident[:])
            mm.then_inc(s_job, 1)
            pe.wait_ge(s_wuh, 1)
            pe.wait_ge(s_wul, 1)
            pe.wait_ge(ld["pool_w"], 16)
            for g in range(G):
                project(("u", g), lambda k: w_u_hi[:, k], w_u_lo, g, x_low=False)
                name = ("pool", g)
                job_free(pe, name)
                pe.wait_ge(s_diff, g + 1)
                pe.matmul(bank(name), w_pool_sb[:, g, :], diff[:, 0:SEQ], start=True, stop=True)
                pe.matmul(bank(name, 1)[:, 0:NS], w_pool_sb[:, g, :], diff[:, SEQ:T], start=True, stop=True).then_inc(s_job, 1)
                name = ("gating", g)
                job_free(pe, name)
                pe.wait_ge(s_v, TT)
                pe.wait_ge(s_emptied["V"], EMPTIED[("blockw", 0)])
                for t in range(LAST):
                    pe.matmul(bank(name)[:, t * P:(t + 1) * P], v_sb[:, t, g * P:(g + 1) * P], wsT[:, g, :], start=True, stop=True)
                pe.matmul(bank(name, 1)[:, 0:NS], v_sb[0:NS, LAST, g * P:(g + 1) * P], block_w[0:NS, g, :],
                          start=True, stop=True).then_inc(s_job, 1)
            pe.wait_ge(ld["w_out"], 16)
            pe.wait_ge(ld["router"], 32)
            pe.wait_ge(s_const, 14)

            def embedding(t):
                name = ("ple", t)
                n = NT[t]
                job_free(pe, name)
                pe.wait_ge(s_emptied["A"], EMPTIED[("pT", t)])
                for b in range(2):
                    for k in range(KP):
                        mm = pe.matmul(bank(name, b)[0:n, :], pT[:, k, t * P:t * P + n], w_proj_sb[:, k, b * 512:(b + 1) * 512],
                                       start=(k == 0), stop=(k == KP - 1))
                mm.then_inc(s_job, 1)

            for i in range(TT + 2):
                if i < TT:
                    name = ("out", i)
                    n = NT[i]
                    job_free(pe, name)
                    for ks in w_z_halves:
                        for b in range(2):
                            for k in range(ks.start, ks.stop):
                                if i == 0 and b == 0:
                                    pe.wait_ge(s_mix, 2 * G - 1 if k < KD - 1 else 2 * G)
                                    if k == KD // 2:
                                        pe.wait_ge(ld["w_out2"], 16)
                                    if k == 3 * KD // 4:
                                        pe.wait_ge(ld["w_out3"], 16)
                                rows_k = ext[:, k, LEAD + i * P:LEAD + i * P + n] if k < G else uT[:, k - G, i * P:i * P + n]
                                w = (w_out_a, w_out_b)[k // (KD // 2)][:, k % (KD // 2), b * 512:(b + 1) * 512]
                                mm = pe.matmul(bank(name, b)[0:n, :], rows_k, w, start=(k == 0), stop=(k == KD - 1),
                                               skip_group_check=True)
                    mm.then_inc(s_job, 1)
                if i == LAST:
                    pe.wait_ge(ld["ple"], 16)
                    pe.wait_ge(ld["p"], 32)
                    for t in range(TT):
                        name = ("pT", t)
                        n = NT[t]
                        job_free(pe, name)
                        for k in range(KP):
                            mm = pe.transpose(bank(name)[:, k * P:k * P + n], p_sb[0:n, t, k * P:(k + 1) * P], ident[0:n, 0:n])
                        mm.then_inc(s_job, 1)
                if i == TT:
                    embedding(0)
                if 0 <= i - 1 < TT:
                    pe.wait_ge(s_xn, TT + i)
                    transposes(("h2T", i - 1), xn[:, (i - 1) % 2, :])
                if 0 <= i - 2 < TT:
                    t = i - 2
                    name = ("logits", t)
                    job_free(pe, name)
                    pe.wait_ge(s_emptied["A"], EMPTIED[("h2T", t)])
                    pe.matmul(bank(name)[:, 0:E], ones[0:1, :], b_router_sb[:], start=True, stop=False)
                    for k in range(KD):
                        mm = pe.matmul(bank(name)[:, 0:E], h2T[:, t % 2, k, :], w_router_sb[:, k, :], start=False, stop=(k == KD - 1))
                    mm.then_inc(s_job, 1)
            embedding(1)
            name = ("rank", 0)
            job_free(pe, name)
            pe.wait_ge(s_mask, TT)
            rk = bank(name)[:, 0:TT * E]
            pe.matmul(rk, before[:], mask[:].rearrange("p t e -> p (t e)"), start=True, stop=False)
            for t in range(LAST):
                n = LAST - t
                mm = pe.matmul(rk[:, (t + 1) * E:].rearrange("p (t e) -> p t e", e=E), ones[:],
                          mask[:, t:t + 1, :].to_broadcast([P, n, E]), start=False, stop=(t == LAST - 1))
            mm.then_inc(s_job, 1)
            name = ("count", 0)
            job_free(pe, name)
            for t in range(TT):
                mm = pe.matmul(bank(name)[:, 0:E], ones[:], mask[:, t, :], start=(t == 0), stop=(t == LAST))
            mm.then_inc(s_job, 1)
            name = ("slots", 0)
            job_free(pe, name)
            pe.wait_ge(s_picks, 1)
            for t in range(TT):
                mm = pe.matmul(bank(name)[:, 0:1], picks[:, t, :], tok_slot[:, 1, t:t + 1], start=(t == 0), stop=(t == LAST))
            mm.then_inc(s_job, 1)
            embedding(2)
            embedding(3)

            pe.wait_ge(s_emptied["A"], TOTAL["A"] - 1)
            pe.wait_ge(s_emptied["V"], TOTAL["V"])

            def slots(u):
                pe.wait_ge(s_picks, u + 1)
                pe.wait_ge(s_rows, u)
                if not (isinstance(u, int) and u <= 2):
                    pe.wait_ge(s_y, u - 2)
                for t in range(TT):
                    mm = pe.matmul(slot_sum, picks[:, t, :], tok_slot[:, 1, t:t + 1], start=(t == 0), stop=(t == LAST))
                mm.then_inc(s_rowps, 1)

            def x_transposes(u):
                pe.wait_ge(s_gather, 16 * u + 16)
                if not (isinstance(u, int) and u <= 1):
                    pe.wait_ge(s_alo, u - 1)
                elif u == 1:
                    pe.wait_ge(s_xlo, 1)
                for k in range(KD):
                    mm = pe.transpose(tp[:, k * P:(k + 1) * P], x_rows[:, k * P:(k + 1) * P], ident[:])
                mm.then_inc(s_xtp, 1)

            def a_transposes(u):
                pe.wait_ge(s_act, u + 1)
                pe.wait_ge(s_xlo, u + 2)
                for k in range(KD):
                    mm = pe.transpose(tp[:, k * P:(k + 1) * P], lin[:, k * P:(k + 1) * P], ident[:])
                mm.then_inc(s_atp, 1)

            def bias(out, oh, lo, hi):
                for c in range(lo, hi, 512):
                    pe.matmul(out[:, c - lo:c - lo + 512], oh[:], bias_hl[:, c:c + 512], start=True, stop=False,
                              skip_group_check=True)

            def hi_products(J, s, out, parts):
                wait_hi(pe, J, s)
                for xs in (0, 1):
                    for xh, xl, base, width in parts:
                        for c in range(0, width, 512):
                            mm = pe.matmul(out[:, c:c + 512], (xh, xl)[xs], w_hi[:, s % SPLIT, base + c:base + c + 512],
                                           start=False, stop=False, skip_group_check=True)
                mm.then_inc(s_hused, 1)

            def lo_products(J, s, out, parts, last):
                wait_lo(pe, J, s)
                for k, (xh, xl, base, width) in enumerate(parts):
                    for c in range(0, width, 512):
                        mm = pe.matmul(out[:, c:c + 512], xh, w_lo[:, s % SPLIT, base + c:base + c + 512],
                                       start=False, stop=last and k == len(parts) - 1, skip_group_check=True)
                mm.then_inc(s_lused, 1)

            def up_start(u):
                pe.wait_ge(s_xhi, u + 1)
                pe.wait_ge(s_xlo, u + 1)
                pe.wait_ge(s_oh, u + 1)
                if not (isinstance(u, int) and u == 0):
                    pe.wait_ge(s_lin, u)
                    pe.wait_ge(s_glu, u)
                bias(gu, oh_up, 0, 2 * FF)

            def up_args(c):
                return gu, [(xT_hi[:, c, :], xT_lo[:, c, :], 0, 2 * FF)]

            def dn_args(c):
                return dn, [(aT_hi[:, 2 * c + j, :], aT_lo[:, 2 * c + j, :], j * D, D) for j in range(2)]

            def up_hi(J, s, c):
                hi_products(J, s, *up_args(c))

            def up_lo(J, s, c):
                lo_products(J, s, *up_args(c), c == UP_CHUNKS - 1)

            def dn_hi(J, s, c):
                hi_products(J, s, *dn_args(c))

            def dn_lo(J, s, c):
                lo_products(J, s, *dn_args(c), c == DN_CHUNKS - 1)

            def dn_start(u, found):
                pe.wait_ge(s_ahi, u + 1)
                pe.wait_ge(s_alo, u + 1)
                pe.wait_ge(s_oh, u + 2)
                pe.wait_ge(s_rows, found)
                if not (isinstance(u, int) and u == 0):
                    pe.wait_ge(s_y, u)
                bias(dn, oh_dn, 2 * FF, 2 * FF + D)

            def step(J, has_dn=True):
                up_start(J + 1)
                for c in range(UP_CHUNKS):
                    up_hi(J, UP_CHUNKS + c, c)
                    if c > 0:
                        up_lo(J, UP_CHUNKS + c - 1, c - 1)
                    elif has_dn:
                        dn_lo(J, UP_CHUNKS - 1, DN_CHUNKS - 1)
                    if c == 1:
                        a_transposes(J)
                    if c == 3:
                        slots(J + 2)
                for c in range(DN_CHUNKS):
                    if c == 0:
                        dn_start(J, J + 3)
                    dn_hi(J, 2 * UP_CHUNKS + c, c)
                    if c > 0:
                        dn_lo(J, 2 * UP_CHUNKS + c - 1, c - 1)
                    else:
                        up_lo(J, 2 * UP_CHUNKS - 1, UP_CHUNKS - 1)
                        x_transposes(J + 2)

            pe.wait_ge(s_bias, 2)
            x_transposes(0)
            embedding(LAST)
            pe.wait_ge(s_emptied["A"], TOTAL["A"])
            up_start(0)
            for c in range(UP_CHUNKS):
                up_hi(0, c, c)
                if c > 0:
                    up_lo(0, c - 1, c - 1)
                if c == 2:
                    slots(1)
            x_transposes(1)
            up_lo(0, UP_CHUNKS - 1, UP_CHUNKS - 1)
            step(0, has_dn=False)
            step(1)
            with pe.Fori(2, E - 1) as J:
                step(J)
            n_over = pe.value_load(over_i[0:1, 0:1], min_val=0, max_val=OVER)
            with pe.If(n_over > 0):
                with pe.Fori(0, OVER) as b:
                    with pe.If(b < n_over):
                        step(b + (E - 1))
            J = n_over + (E - 1)
            a_transposes(J)
            dn_lo(J, UP_CHUNKS - 1, DN_CHUNKS - 1)
            dn_start(J, J + 2)
            for c in range(DN_CHUNKS):
                dn_hi(J, UP_CHUNKS + c, c)
                if c > 0:
                    dn_lo(J, UP_CHUNKS + c - 1, c - 1)
            dn_lo(J, UP_CHUNKS + DN_CHUNKS - 1, DN_CHUNKS - 1)

            pe.wait_ge(s_y, n_over + E)

            def x2_transposes(t):
                pe.wait_ge(s_comb, t + 1)
                if t >= 2:
                    pe.wait_ge(s_x2l, t - 1)
                for k in range(KD):
                    mm = pe.transpose(ps[:, 4 + 2 * (t % 2) + k // 4, (k % 4) * P:(k % 4 + 1) * P],
                                      resid[:, t, k * P:(k + 1) * P], ident[:])
                mm.then_inc(s_x2tp, 1)

            x2_transposes(0)
            for t in range(TT):
                gate_hi_products(pe, t)
                if t < LAST:
                    x2_transposes(t + 1)
                gate_low_products(pe, t)

        @block.vector
        def _(dve):
            chain = [0]

            def link(ins):
                chain[0] += 1
                ins.then_inc(s_chain, 1)
                dve.wait_ge(s_chain, chain[0])

            dve.wait_ge(s_ident, 1)
            link(dve.tensor_copy(rep[0:DS, :].rearrange("p (b s) -> p b s", b=DB),
                                 ident[0:DS, 0:DS].rearrange("p (o s) -> p o s", o=1).to_broadcast([DS, DB, DS])))
            dve.wait_ge(ld["gain"], 16)
            for t in range(TT):
                dve.wait_ge(s_sq, t + 1)
                dve.tensor_scalar(var1[:, t:t + 1], sq1[:, t:t + 1], 1.0 / D, NORM_EPS, ALU.mult, ALU.add).then_inc(s_var, 1)
                dve.wait_ge(s_rstd, t + 1)
                if t >= 2:
                    job_filled(dve, ("xT", t - 2))
                dve.scalar_tensor_tensor(out=xn[:, t % 2, :], in0=resid[:, t, :], scalar=rstd1[:, t:t + 1], in1=gain[:],
                                         op0=ALU.mult, op1=ALU.mult).then_inc(s_xn, 1)
            def layernorm_stats(t):
                n = NT[t]
                dve.wait_ge(s_emptied["A"], EMPTIED[("v", t)])
                for h in range(G):
                    ins = dve.bn_stats(stats[0:n, h, :], v_sb[0:n, t, h * P:(h + 1) * P])
                link(ins)
                for h in range(G):
                    ins = dve.bn_aggr(mean_var[0:n, t, h, :], stats[0:n, h, :])
                link(ins)
                dve.tensor_scalar(ln_var[0:n, t, :], mean_var[0:n, t, :, 1], LN_EPS, None, ALU.add).then_inc(s_lnv, 1)

            def difference(g):
                w = 1.0 / WINDOWS[g]
                dve.wait_ge(s_sum, g + 1)
                if g >= 1:
                    job_filled(dve, ("pool", g - 1))
                link(dve.tensor_tensor(sumA[:, LEAD:2 * LEAD], sumA[:, LEAD:2 * LEAD], head_fix[:, g, :], ALU.mult))
                dve.scalar_tensor_tensor(out=diff[:, 0:SEQ], in0=sumA[:, LEAD:LEAD + SEQ], scalar=w,
                                         in1=ext[:, g, LEAD:LEAD + SEQ], op0=ALU.mult, op1=ALU.subtract)

                def new(a):
                    return a.rearrange("p (b s) -> p b s", b=DB)[:, :, LEAD:]
                dve.scalar_tensor_tensor(out=diff[:, SEQ:T].rearrange("p (b s) -> p b s", b=DB),
                                         in0=new(sumA[:, LEAD + SEQ:]), scalar=w, in1=new(ext[:, g, LEAD + SEQ:]),
                                         op0=ALU.mult, op1=ALU.subtract).then_inc(s_diff, 1)

            def pool_out(g):
                name = ("pool", g)
                job_filled(dve, name)
                dve.tensor_scalar(ext[:, g, LEAD:LEAD + SEQ], bank(name), scaleT[:, g:g + 1], None, ALU.mult).then_inc(s_mix, 1)
                dve.tensor_scalar(ext[:, g, LEAD + SEQ:LEAD + T], bank(name, 1)[:, 0:NS], scaleT[:, g:g + 1], None,
                                  ALU.mult).then_inc(s_emptied["V"], 1)

            def layernorm_apply(t):
                n = NT[t]
                dve.wait_ge(s_lnr, t + 1)
                for h in range(G):
                    v = v_sb[0:n, t, h * P:(h + 1) * P]
                    ins = dve.tensor_scalar(v, v, mean_var[0:n, t, h, 0:1], ln_rstd[0:n, t, h:h + 1], ALU.subtract, ALU.mult)
                link(ins)
                v = v_sb[0:n, t, :]
                link(dve.tensor_tensor(v, v, ln_g[0:n, :], ALU.mult))
                dve.tensor_tensor(v, v, ln_b[0:n, :], ALU.add).then_inc(s_v, 1)

            def gating_out(g):
                name = ("gating", g)
                job_filled(dve, name)
                if g >= 1:
                    dve.wait_ge(s_mix, 2 * g)
                dve.tensor_tensor(gated[:, 0:SEQ].rearrange("p (t n) -> p t n", n=P),
                                  bank(name).rearrange("p (t n) -> p t n", n=P),
                                  sgu_bias[:, g:g + 1, :].to_broadcast([P, LAST, P]), ALU.add)
                dve.tensor_tensor(gated[:, SEQ:].rearrange("p (b s) -> p b s", b=DB),
                                  bank(name, 1)[:, 0:NS].rearrange("p (b s) -> p b s", b=DB),
                                  sgu_bias[:, g:g + 1, 0:DS].to_broadcast([P, DB, DS]), ALU.add).then_inc(s_emptied["V"], 1)
                dve.wait_ge(s_emptied["V"], EMPTIED[name])
                dve.wait_ge(s_emptied["A"], EMPTIED[("u", g)])
                dve.tensor_tensor(uT[:, g, :], gated[:], uT[:, g, :], ALU.mult).then_inc(s_mix, 1)


            dve.wait_ge(ld["ln"], 32)
            layernorm_stats(0)
            layernorm_apply(0)
            for i, ks in enumerate(w_z_halves):
                dve.wait_ge(s_wzh, i + 1)
                dve.tensor_tensor(w_z_lo[:, ks, :], w_z_sb[:, ks, :], w_z_hi[i][:].bitcast(F32), ALU.subtract).then_inc(s_wzl, 1)
            name = ("misc", 0)
            job_filled(dve, name)
            dve.wait_ge(s_ext0, 2)
            dve.tensor_copy(wsT[:].rearrange("p h i -> p (h i)"), bank(name))
            n = DB * PB
            for g in range(G):
                dve.tensor_copy(ext[:, g, LEAD + SEQ:].rearrange("p (b s) -> p b s", b=DB)[:, :, 1:LEAD],
                                bank(name, 1)[:, g * n:(g + 1) * n].rearrange("p (b r) -> p b r", b=DB))
            dve.tensor_copy(scaleT[:], bank(name, 1)[:, G * n:G * n + G]).then_inc(s_emptied["V"], 1)
            layernorm_stats(1)
            layernorm_apply(1)
            name = ("blockw", 0)
            job_filled(dve, name)
            dve.wait_ge(s_wpart, 2)
            for h in range(G):
                few = bank(name)[0:NS, h * DS:(h + 1) * DS].rearrange("p (o s) -> p o s", o=1).to_broadcast([NS, DB, DS])
                ins = dve.tensor_tensor(block_w[0:NS, h, :].rearrange("p (b s) -> p b s", b=DB), few, same_seq[0:NS], ALU.mult)
            ins.then_inc(s_emptied["V"], 1)
            dve.wait_ge(s_const, 1 + G)
            link(dve.reciprocal(head_fix[:], head_fix[:]))
            for g, w in enumerate(WINDOWS):
                ins = dve.tensor_scalar(head_fix[:, g, :], head_fix[:, g, :], float(w), None, ALU.mult)
            link(ins)
            layernorm_stats(2)
            job_filled(dve, ("v", LAST))
            dve.wait_ge(s_xh, TT)
            for k in range(KD):
                dve.tensor_tensor(xTl[:, k, 0:T], xT[:, k, 0:T], xTh[:, k, :].bitcast(F32), ALU.subtract).then_inc(s_xl, 1)
            layernorm_apply(2)
            layernorm_stats(3)
            layernorm_apply(3)
            dve.wait_ge(s_wuh, 1)
            dve.tensor_tensor(w_u_lo[:], w_u_sb[:], w_u_hi[:].bitcast(F32), ALU.subtract).then_inc(s_wul, 1)
            layernorm_stats(4)
            layernorm_apply(4)
            dve.wait_ge(ld["small"], 16)
            difference(0)
            for g in range(G):
                pool_out(g)
                if g < G - 1:
                    difference(g + 1)
                gating_out(g)

            def logits_top(t):
                name = ("logits", t)
                job_filled(dve, name)
                dve.tensor_copy(logits[:, t, :], bank(name)[:, 0:E]).then_inc(s_emptied["V"], 1)
                dve.wait_ge(s_emptied["V"], EMPTIED[name])
                link(dve.max(top8[:, t, :], logits[:, t, :]))
                link(dve.max_index(top_i[:, t, :], top8[:, t, :], logits[:, t, :]))
                dve.tensor_scalar(neg_max[:, t:t + 1], top8[:, t, 0:1], -1.0, None, ALU.mult).then_inc(s_top, 1)
                link(dve.tensor_copy(top_f[:, t, :], top_i[:, t, 0:TOPK]))
                link(dve.tensor_tensor(chosen[:, t, :, :],
                                       expert_iota[:].rearrange("p (o e) -> p o e", o=1).to_broadcast([P, TOPK, E]),
                                       top_f[:, t, :].rearrange("p (k o) -> p k o", o=1).to_broadcast([P, TOPK, E]),
                                       ALU.is_equal))
                dve.tensor_reduce(mask[0:NT[t], t, :], chosen[0:NT[t], t, :, :].rearrange("p k e -> p e k"), AX.X,
                                  ALU.add).then_inc(s_mask, 1)

            dve.wait_ge(ld["gain2"], 16)
            dve.wait_ge(s_const, 14)
            for i in range(TT + 2):
                if i < TT:
                    name = ("out", i)
                    job_filled(dve, name)
                    for b in range(2):
                        x = resid[0:NT[i], i, b * 512:(b + 1) * 512]
                        ins = dve.tensor_tensor(x, x, bank(name, b)[0:NT[i], :], ALU.add)
                    ins.then_inc(s_emptied["V"], 1)
                if 0 <= i - 2 < TT:
                    logits_top(i - 2)
                if i < TT:
                    dve.wait_ge(s_sq, TT + i + 1)
                    dve.tensor_scalar(var2[:, i:i + 1], sq2[:, i:i + 1], 1.0 / D, NORM_EPS, ALU.mult, ALU.add).then_inc(s_var, 1)
                    dve.wait_ge(s_rstd, TT + i + 1)
                    if i >= 2:
                        job_filled(dve, ("h2T", i - 2))
                        dve.wait_ge(s_xrow[i - 2], 16)
                    dve.scalar_tensor_tensor(out=xn[:, i % 2, :], in0=resid[:, i, :], scalar=rstd2[:, i:i + 1], in1=gain2[:],
                                             op0=ALU.mult, op1=ALU.mult).then_inc(s_xn, 1)
                if i == 2:
                    dve.wait_ge(s_bias_hi, 1)
                    dve.tensor_tensor(bias_hl[E:2 * E, :], bias_raw[E:2 * E, :], bias_hl[E:2 * E, :].bitcast(F32),
                                      ALU.subtract).then_inc(s_bias, 1)
            def lo_part(J, s):
                wait_split_used(dve, s_lused, J, s)
                wait_hi(dve, J, s)
                dve.tensor_tensor(w_lo[:, s % SPLIT, :], raw[:, s % RING, :], w_hi[:, s % SPLIT, :].bitcast(F32),
                                  ALU.subtract).then_inc(s_lo["V"], 1)

            link(dve.tensor_tensor(chosen_row[:], chosen[:],
                                   row_code[:].rearrange("p t (k o) -> p t k o", o=1).to_broadcast([P, TT, TOPK, E]), ALU.mult))
            for t in range(TT):
                ins = dve.tensor_reduce(pos_row[:, 1, t, :], chosen_row[:, t].rearrange("p k e -> p e k"), AX.X, ALU.add)
            link(ins)
            link(dve.memset(rows[:], NO_ROW))
            lo_part(0, 0)
            name = ("rank", 0)
            job_filled(dve, name)
            dve.tensor_copy(rank[:].rearrange("p t e -> p (t e)"), bank(name)[:, 0:TT * E]).then_inc(s_emptied["V"], 1)
            dve.wait_ge(s_emptied["V"], EMPTIED[name])
            dve.tensor_copy(tok_slot[:, 1, :], pos_row[:, 1, :, 0])
            link(dve.scalar_tensor_tensor(out=tok_slot[:, 0, :], in0=rank[:, :, 0], scalar=1.0, in1=mask[:, :, 0],
                                          op0=ALU.add, op1=ALU.mult))
            for t in range(TT):
                ins = dve.tensor_scalar(picks[:, t, :], slot1[:], tok_slot[:, 0, t:t + 1], None, ALU.is_equal)
            ins.then_inc(s_picks, 1)
            name = ("count", 0)
            job_filled(dve, name)
            dve.tensor_copy(count[:], bank(name)[:, 0:E]).then_inc(s_emptied["V"], 1)
            dve.wait_ge(s_emptied["V"], EMPTIED[name])
            link(dve.tensor_scalar(over[:], count[:], float(P + 1), None, ALU.is_ge))
            link(dve.tensor_scalar(depth[:], rank[:], float(P), None, ALU.is_ge))
            link(dve.tensor_copy(first[:], depth[:]))
            job_filled(dve, ("slots", 0))
            dve.tensor_scalar(rows[:, 0:1], bank(("slots", 0))[:, 0:1], float(NO_ROW), None, ALU.add).then_inc(s_emptied["V"], 1)
            dve.wait_ge(s_emptied["V"], EMPTIED[("slots", 0)])
            dve.tensor_scalar(token_of[:], rows[:, 0:1], 2, None, ALU.logical_shift_right).then_inc(s_rows, 1)
            lo_part(0, 1)
            for m in range(2, TT):
                dve.scalar_tensor_tensor(out=over[:], in0=count[:], scalar=float(m * P + 1), in1=over[:],
                                         op0=ALU.is_ge, op1=ALU.add)
                link(dve.scalar_tensor_tensor(out=depth[:], in0=rank[:], scalar=float(m * P), in1=depth[:],
                                              op0=ALU.is_ge, op1=ALU.add))
            link(dve.tensor_tensor_scan(over_end[:], ones[:, 0:E], over[:], 0.0, ALU.mult, ALU.add))
            dve.tensor_copy(over_i[:], over_end[:, E - 1:E])
            link(dve.tensor_tensor(over_from[:], over_end[:], over[:], ALU.subtract))
            link(dve.tensor_tensor(over_from[:], over_from[:], expert_iota[:], ALU.subtract))
            link(dve.tensor_scalar(over_from[:], over_from[:], float(E - 1), None, ALU.add))

            def by_tile(a):
                return a.rearrange("p (o e) -> p o e", o=1).to_broadcast([P, TT, E])
            link(dve.tensor_tensor(first[:], first[:], by_tile(over_from[:]), ALU.mult))
            link(dve.tensor_tensor(first[:], first[:], depth[:], ALU.add))
            link(dve.tensor_tensor(first[:], first[:], by_tile(expert_iota[:]), ALU.add))
            link(dve.scalar_tensor_tensor(out=first[:], in0=first[:], scalar=1.0, in1=mask[:], op0=ALU.add, op1=ALU.mult))
            link(dve.tensor_scalar(block_of[:], first[:], -1.0, None, ALU.add))
            link(dve.scalar_tensor_tensor(out=pos_row[:, 0], in0=depth[:], scalar=float(-P), in1=rank[:], op0=ALU.mult, op1=ALU.add))
            link(dve.tensor_scalar(pos_row[:, 0], pos_row[:, 0], 1.0, None, ALU.add))
            LINKS = 5 + 2 + 1
            moe = {"base": 0, "n": 0}

            def mlink(ins):
                moe["n"] += 1
                ins.then_inc(s_chain, 1)
                dve.wait_ge(s_chain, moe["base"] + moe["n"])

            def find(u):
                mlink(dve.tensor_scalar(same_block[:], block_of[:], cur_block[:, 0:1], None, ALU.is_equal))
                mlink(dve.tensor_tensor(in_block[:], pos_row[:],
                                        same_block[:].rearrange("p (o t) e -> p o t e", o=1).to_broadcast([P, 2, TT, E]), ALU.mult))
                mlink(dve.tensor_reduce(tok_slot[:], in_block[:], AX.X, ALU.add))
                for t in range(TT):
                    ins = dve.tensor_scalar(picks[:, t, :], slot1[:], tok_slot[:, 0, t:t + 1], None, ALU.is_equal)
                ins.then_inc(s_picks, 1)

            def next_expert(u):
                mlink(dve.scalar_tensor_tensor(out=junk_b[:], in0=block_iota[:], scalar=cur_block[:, 0:1], in1=block_expert[:],
                                               op0=ALU.is_equal, op1=ALU.mult, accum_out=cur_expert[:]))
                mlink(dve.tensor_scalar(cur_block[:], cur_block[:], 1.0, None, ALU.add))

            def row_numbers(u):
                dve.wait_ge(s_rowps, u)
                dve.wait_ge(s_gather, 16 * u)
                mlink(dve.tensor_copy(rows_tmp[:], rows[:, 0:3]))
                dve.tensor_copy(rows[:, 1:4], rows_tmp[:])
                mlink(dve.tensor_scalar(rows[:, 0:1], slot_sum, float(NO_ROW), None, ALU.add))
                dve.tensor_scalar(token_of[:], rows[:, 0:1], 2, None, ALU.logical_shift_right).then_inc(s_rows, 1)

            def bias_picks(u):
                mlink(dve.tensor_copy(oh_dn[:], oh_up[:].bitcast(F32)))
                dve.tensor_scalar(oh_up[:], bias_row[:, 0:1].to_broadcast([P, P]), cur_expert[:, 0:1], None,
                                  ALU.is_equal).then_inc(s_oh, 1)

            def xT_low(u):
                dve.wait_ge(s_xhi, u + 1)
                dve.tensor_tensor(xT_lo[:].rearrange("p k n -> p (k n)"), tp, xT_hi[:].rearrange("p k n -> p (k n)").bitcast(F32),
                                  ALU.subtract).then_inc(s_xlo, 1)

            def aT_low(u):
                dve.wait_ge(s_ahi, u + 1)
                dve.tensor_tensor(aT_lo[:].rearrange("p k n -> p (k n)"), tp, aT_hi[:].rearrange("p k n -> p (k n)").bitcast(F32),
                                  ALU.subtract).then_inc(s_alo, 1)

            def clamps(u, chunks):
                dve.wait_ge(s_lused, chunks)
                dve.tensor_scalar(glu[:], gu[:, 0:FF], LIMIT, None, ALU.min).then_inc(s_glu, 1)
                dve.tensor_scalar(lin[:], gu[:, FF:], LIMIT, -LIMIT, ALU.min, ALU.max).then_inc(s_lin, 1)

            def activation(u):
                dve.wait_ge(s_gs, u + 1)
                dve.wait_ge(s_lin, u + 1)
                dve.scalar_tensor_tensor(out=lin[:], in0=lin[:], scalar=1.0, in1=sig[:], op0=ALU.add,
                                         op1=ALU.mult).then_inc(s_act, 1)

            def step(J, first=False):
                moe["n"] = 0
                for x in range(STEP_CHUNKS):
                    s = UP_CHUNKS + x
                    if x == 1 and first:
                        activation(0)
                    if x == 2:
                        find(J + 2)
                        next_expert(J + 2)
                    if lo_by(s) == "V":
                        lo_part(J, s)
                    if x == 4:
                        aT_low(J)
                    if x == 6:
                        row_numbers(J + 2)
                    if x == 10:
                        clamps(J + 1, STEP_CHUNKS * J + 2 * UP_CHUNKS)
                activation(J + 1)
                bias_picks(J + 2)
                xT_low(J + 2)
                assert moe["n"] == LINKS

            moe["base"] = chain[0]
            dve.tensor_copy(block_expert[:, 0:E], expert_iota[:])
            mlink(dve.tensor_tensor(over_cmp[:], over_end[:].rearrange("p (o e) -> p o e", o=1).to_broadcast([P, OVER + 2, E]),
                                   block_iota[:, 0:OVER + 2].rearrange("p (b o) -> p b o", o=1).to_broadcast([P, OVER + 2, E]),
                                   ALU.is_le))
            mlink(dve.tensor_reduce(block_expert[:, E:], over_cmp[:], AX.X, ALU.add))
            dve.tensor_copy(block_expert_i[:], block_expert[:]).then_inc(s_route, 1)
            dve.wait_ge(s_route, 1)
            mlink(dve.memset(oh_up[:].bitcast(F32), 0.0))
            next_expert(0)
            dve.wait_ge(s_exp, TT)
            mlink(dve.reciprocal(exp_rcp[:], exp_sum[:]))
            dve.tensor_tensor(topw[:], exps[:], exp_rcp[:].rearrange("p (t o) -> p t o", o=1).to_broadcast([P, TT, TOPK]), ALU.mult)

            bias_picks(0)
            xT_low(0)
            dve.wait_ge(s_emptied["A"], TOTAL["A"])
            lo_part(0, 2)
            find(1)
            next_expert(1)
            for s in range(3, UP_CHUNKS):
                if lo_by(s) == "V":
                    lo_part(0, s)
                if s == 3:
                    row_numbers(1)
            clamps(0, UP_CHUNKS)
            bias_picks(1)
            xT_low(1)
            before_steps = moe["base"] + moe["n"]
            moe["base"] = before_steps
            step(0, first=True)
            moe["base"] = before_steps + LINKS
            step(1)
            with dve.Fori(2, E - 1) as J:
                moe["base"] = J * LINKS + before_steps
                step(J)
            n_over = dve.value_load(over_i[0:1, 0:1], min_val=0, max_val=OVER)
            with dve.If(n_over > 0):
                with dve.Fori(0, OVER) as b:
                    with dve.If(b < n_over):
                        moe["base"] = (b + (E - 1)) * LINKS + before_steps
                        step(b + (E - 1))
            J = n_over + (E - 1)
            for x in range(3):
                if lo_by(UP_CHUNKS + x) == "V":
                    lo_part(J, UP_CHUNKS + x)
                if x == 0:
                    aT_low(J)
            if lo_by(UP_CHUNKS + 3) == "V":
                lo_part(J, UP_CHUNKS + 3)

            dve.wait_ge(s_lused, n_over * STEP_CHUNKS + E * STEP_CHUNKS)
            for c in range(DN_CHUNKS):
                dve.wait_ge(s_ghi, c + 1)
                dve.tensor_tensor(gate_lo[:, 2 * c:2 * c + 2, :].rearrange("p j n -> p (j n)"), raw[:, c, :],
                                  gate_hi[c][:].rearrange("p j n -> p (j n)").bitcast(F32), ALU.subtract).then_inc(s_glo, 1)
            dve.wait_ge(ld["gain_f"], 16)
            tail = [0]

            def tlink(ins):
                tail[0] += 1
                ins.then_inc(s_tchain, 1)
                dve.wait_ge(s_tchain, tail[0])

            def combine(t):
                n = NT[t]
                x = resid[0:n, t, :]
                i = YK_SLOT[t % YB]
                yk = raw[0:n, i:i + 2, :].rearrange("p a (b d) -> p (a b) d", d=D)
                for k in range(TOPK):
                    if k % 2 == 0:
                        dve.wait_ge(s_yk[t % YB][k // 2], 16 * (t // YB + 1))
                    ins = dve.scalar_tensor_tensor(out=x, in0=yk[:, k, :], scalar=topw[0:n, t, k:k + 1], in1=x,
                                                   op0=ALU.mult, op1=ALU.add)
                    if k < TOPK - 1:
                        tlink(ins)
                ins.then_inc(s_comb, 1)

            def finish(t):
                dve.wait_ge(s_gate, t + 1)
                dve.wait_ge(s_x2tp, t + 1)
                n = NT[t]
                g = gate[0:n, t % 2, :]
                tlink(dve.tensor_tensor(g, g, ple[0:n, t, :], ALU.mult))
                dve.tensor_tensor(resid[0:n, t, :], resid[0:n, t, :], g, ALU.add).then_inc(s_x3, 1)
                dve.wait_ge(s_sq3, t + 1)
                dve.tensor_scalar(var3[:, t:t + 1], sq3[:, t:t + 1], 1.0 / D, NORM_EPS, ALU.mult, ALU.add).then_inc(s_var3, 1)
                dve.wait_ge(s_rstd3, t + 1)
                if t >= 2:
                    dve.wait_ge(s_ost[t % 2], 16 * (t // 2))
                dve.scalar_tensor_tensor(out=out_rows[:, t % 2, :], in0=resid[:, t, :], scalar=rstd3[:, t:t + 1], in1=gain_f[:],
                                         op0=ALU.mult, op1=ALU.mult).then_inc(s_orow, 1)

            def x2_low(t):
                dve.wait_ge(s_x2h, t + 1)
                dve.tensor_tensor(x2T_lo[:, t % 2].rearrange("p k n -> p (k n)"),
                                  ps[:, 4 + 2 * (t % 2):6 + 2 * (t % 2), :].rearrange("p a n -> p (a n)"),
                                  x2T_hi[:, t % 2].rearrange("p k n -> p (k n)").bitcast(F32), ALU.subtract).then_inc(s_x2l, 1)

            for t in range(TT):
                combine(t)
                if t >= 1:
                    x2_low(t - 1)
                if t >= 2:
                    finish(t - 2)
            x2_low(LAST)
            finish(LAST - 1)
            finish(LAST)


_INS = ["x_prompt", "x_sample", "state_pool", "p_prompt", "p_sample", "norm_mix", "w_in", "w_pool", "pool_scale",
        "sgu_ln_g", "sgu_ln_b", "sgu_w", "sgu_b", "w_out", "norm_ffn", "w_router", "b_router", "w_up", "b_up",
        "w_down", "b_down", "w_ple_gate", "w_ple_proj", "norm_final"]
_OUTS = [(1, 512, 1024), (8, 4, 1024), (1, 1, 15, 512), (1, 8, 15, 512), (1, 8, 4, 512)]


def kernel(**inputs):
    import numpy as _np
    import concourse.bacc as _bacc
    from concourse import mybir as _mybir
    from concourse.bass_utils import run_bass_kernel_spmd as _run

    nc = _bacc.Bacc("TRN2", target_bir_lowering=False, num_devices=1)
    arrays, args = {}, []
    for name in _INS:
        a = _np.ascontiguousarray(inputs[name])
        arrays[f"in_{name}_dram"] = a
        args.append(nc.dram_tensor(f"in_{name}_dram", a.shape, _mybir.dt.from_np(a.dtype), kind="ExternalInput").ap())
    for i, shape in enumerate(_OUTS):
        args.append(nc.dram_tensor(f"out_{i}_dram", shape, _mybir.dt.from_np(_np.dtype("float32")), kind="ExternalOutput").ap())
    build(nc, *args)
    r = _run(nc, [arrays], core_ids=[0])
    return tuple(r.results[0][f"out_{i}_dram"] for i in range(len(_OUTS)))
```
